# Optimizing a Trainium2 kernel written in Bass

```python
import math
import jax, jax.numpy as jnp
from jax import lax
import numpy as np

D_MODEL = 1024
BATCH = 1
SEQ = 128
DEPTH = 2
DEC_BATCH = 1
DEC_SEQ = 256
PAST_LEN = 128

GRID_W = 64
HEAD_DIM = 64
A_HEADS = 4
A_KV = 2
WINDOW = 128
B_HEADS = 4
B_KV = 2
Q_BLOCK = 128
ROPE_THETA = 10000.0
ROPE_QUARTER = HEAD_DIM // 4
SSM_HEADS = 8
SSM_HEAD_DIM = 64
D_SSM = SSM_HEADS * SSM_HEAD_DIM
SSM_GROUPS = 2
SSM_STATE = 64
CONV_W = 3
CHUNK = 128
XBC_DIM = D_SSM + 2 * SSM_GROUPS * SSM_STATE
D_MIX = A_HEADS * HEAD_DIM + B_HEADS * HEAD_DIM + D_SSM
IN_SIZES = (A_HEADS * HEAD_DIM, A_KV * HEAD_DIM, A_KV * HEAD_DIM,
            B_HEADS * HEAD_DIM, B_KV * HEAD_DIM, B_KV * HEAD_DIM,
            D_SSM, XBC_DIM, 2 * SSM_HEADS)
D_IN = (A_HEADS + 2 * A_KV + B_HEADS + 2 * B_KV) * HEAD_DIM + D_SSM + XBC_DIM + 2 * SSM_HEADS
N_EGROUPS = 4
EXPERTS_PER_GROUP = 4
N_EXPERTS = N_EGROUPS * EXPERTS_PER_GROUP
TOP_K_IN_GROUP = 2
D_EXPERT = 256
EPS = 1e-6

kernel_name = 'hymba_prefix_diffusion_step'

f32 = jnp.float32

def rmsnorm(x, g):
    xf = x.astype(f32)
    y = xf * lax.rsqrt(jnp.mean(xf * xf, axis=-1, keepdims=True) + EPS)
    return y.astype(x.dtype) * g

def modulate(h, shift, scale):
    return h * (1 + scale) + shift

def axial_rope_tables(n_rows):
    rows = jnp.repeat(jnp.arange(n_rows), GRID_W).astype(f32)
    cols = jnp.tile(jnp.arange(GRID_W), n_rows).astype(f32)
    inv = ROPE_THETA ** (-jnp.arange(ROPE_QUARTER, dtype=f32) / ROPE_QUARTER)
    ang_r = rows[:, None] * inv
    ang_c = cols[:, None] * inv
    ang = jnp.concatenate([ang_r, ang_r, ang_c, ang_c], axis=-1)
    return jnp.cos(ang), jnp.sin(ang)

def apply_rope(x, cos, sin):
    x0, x1, x2, x3 = jnp.split(x, 4, axis=-1)
    rot = jnp.concatenate([-x1, x0, -x3, x2], axis=-1)
    c = cos.astype(x.dtype)[None, :, None, :]
    s = sin.astype(x.dtype)[None, :, None, :]
    return x * c + rot * s

def softmax_with_sink(s, sink):
    if sink is None:
        return jax.nn.softmax(s, axis=-1)
    kv, g = s.shape[-4], s.shape[-3]
    sk = jnp.broadcast_to(sink.astype(f32).reshape(kv, g, 1, 1), s.shape[:-1] + (1,))
    p = jax.nn.softmax(jnp.concatenate([s, sk], axis=-1), axis=-1)
    return p[..., :-1]

def attend_blocks(q, k, v, sink):
    b, n, h, d = q.shape
    kv = k.shape[2]
    g = h // kv
    nb = n // Q_BLOCK
    qb = q.reshape(b, nb, Q_BLOCK, kv, g, d).transpose(1, 0, 2, 3, 4, 5)

    def one_block(qblk):
        s = jnp.einsum('bqkgd,bskd->bkgqs', qblk, k).astype(f32) * (d ** -0.5)
        p = softmax_with_sink(s, sink)
        return jnp.einsum('bkgqs,bskd->bqkgd', p.astype(v.dtype), v)

    o = lax.map(one_block, qb)
    return o.transpose(1, 0, 2, 3, 4, 5).reshape(b, n, h, d)

def banded_attention(q, k, v, k_ctx, v_ctx, sink):
    b, n, h, d = q.shape
    kv = k.shape[2]
    g = h // kv
    W = WINDOW
    nb = n // W
    pad = ((0, 0), (W, W), (0, 0), (0, 0))
    kp = jnp.pad(k, pad).reshape(b, nb + 2, W, kv, d)
    vp = jnp.pad(v, pad).reshape(b, nb + 2, W, kv, d)
    kband = jnp.concatenate([kp[:, :-2], kp[:, 1:-1], kp[:, 2:]], axis=2)
    vband = jnp.concatenate([vp[:, :-2], vp[:, 1:-1], vp[:, 2:]], axis=2)
    qb = q.reshape(b, nb, W, kv, g, d)
    scale = d ** -0.5
    s_loc = jnp.einsum('bnqkgd,bnskd->bnkgqs', qb, kband).astype(f32) * scale
    s_ctx = jnp.einsum('bnqkgd,bskd->bnkgqs', qb, k_ctx).astype(f32) * scale
    blk = jnp.arange(nb)[:, None, None]
    qi = blk * W + jnp.arange(W)[None, :, None]
    ki = (blk - 1) * W + jnp.arange(3 * W)[None, None, :]
    valid = (jnp.abs(ki - qi) <= W) & (ki >= 0) & (ki < n)
    s_loc = jnp.where(valid[None, :, None, None, :, :], s_loc, -jnp.inf)
    p = softmax_with_sink(jnp.concatenate([s_loc, s_ctx], axis=-1), sink)
    p_loc = p[..., :3 * W].astype(v.dtype)
    p_ctx = p[..., 3 * W:].astype(v.dtype)
    o = (jnp.einsum('bnkgqs,bnskd->bnqkgd', p_loc, vband)
         + jnp.einsum('bnkgqs,bskd->bnqkgd', p_ctx, v_ctx))
    return o.reshape(b, n, h, d)

def conv_centred(x, w, bias):
    c = x.shape[-1]
    y = lax.conv_general_dilated(x, w[:, None, :].astype(x.dtype), window_strides=(1,),
                                 padding=[(CONV_W // 2, CONV_W // 2)],
                                 dimension_numbers=('NWC', 'WIO', 'NWC'), feature_group_count=c)
    return y + bias

def ssd_chunked(x, dt, a, bm, cm, h0):
    b, l, h, p = x.shape
    g = bm.shape[2]
    nc = l // CHUNK
    rep = h // g
    x = x.astype(f32)
    dt = dt.astype(f32)
    bm = jnp.repeat(bm.astype(f32), rep, axis=2).reshape(b, nc, CHUNK, h, -1)
    cm = jnp.repeat(cm.astype(f32), rep, axis=2).reshape(b, nc, CHUNK, h, -1)
    xd = (x * dt[..., None]).reshape(b, nc, CHUNK, h, p)
    da = (dt * a).reshape(b, nc, CHUNK, h).transpose(0, 3, 1, 2)
    cs = jnp.cumsum(da, axis=-1)
    seg = cs[..., :, None] - cs[..., None, :]
    lower = jnp.tril(jnp.ones((CHUNK, CHUNK), dtype=bool))
    lmat = jnp.exp(jnp.where(lower, seg, -jnp.inf))
    scores = jnp.einsum('bclhn,bcshn->bhcls', cm, bm) * lmat
    y_diag = jnp.einsum('bhcls,bcshp->bclhp', scores, xd)
    decay_to_end = jnp.exp(cs[..., -1:] - cs)
    chunk_states = jnp.einsum('bclhn,bhcl,bclhp->bchpn', bm, decay_to_end, xd)
    chunk_decay = jnp.exp(cs[..., -1])

    def step(hc, inp):
        st, dec = inp
        return hc * dec[..., None, None] + st, hc

    h_final, h_enter = lax.scan(step, h0.astype(f32),
                                (chunk_states.transpose(1, 0, 2, 3, 4), chunk_decay.transpose(2, 0, 1)))
    h_enter = h_enter.transpose(1, 0, 2, 3, 4)
    y_off = jnp.einsum('bclhn,bchpn,bhcl->bclhp', cm, h_enter, jnp.exp(cs))
    return (y_diag + y_off).reshape(b, l, h, p), h_final

def mamba_mix(z, xbc, dt_raw, conv_w, conv_b, dt_bias, a_log, d_skip, ssm_g, h0_f, h0_b):
    b, n, _ = xbc.shape
    xbc = jax.nn.silu(conv_centred(xbc, conv_w, conv_b))
    xs, bm, cm = jnp.split(xbc, [D_SSM, D_SSM + SSM_GROUPS * SSM_STATE], axis=-1)
    xs = xs.reshape(b, n, SSM_HEADS, SSM_HEAD_DIM)
    bm = bm.reshape(b, n, SSM_GROUPS, SSM_STATE)
    cm = cm.reshape(b, n, SSM_GROUPS, SSM_STATE)
    dt = jax.nn.softplus(dt_raw.astype(f32).reshape(b, n, 2, SSM_HEADS) + dt_bias.astype(f32))
    a = -jnp.exp(a_log.astype(f32))
    rev = lambda t: jnp.flip(t, axis=1)
    y_f, h_f = ssd_chunked(xs, dt[:, :, 0], a[0], bm, cm, h0_f)
    y_b, h_b = ssd_chunked(rev(xs), rev(dt[:, :, 1]), a[1], rev(bm), rev(cm), h0_b)
    y = y_f + rev(y_b) + xs.astype(f32) * d_skip.astype(f32)[:, None]
    y = y.astype(z.dtype).reshape(b, n, D_SSM)
    return rmsnorm(y * jax.nn.silu(z), ssm_g), h_f, h_b

def mix_layer(h, w_in, a_sink, q_norm_g, k_norm_g, conv_w, conv_b, dt_bias, a_log, d_skip, ssm_norm_g,
              w_out, cache):
    b, n, _ = h.shape
    points = np.cumsum(IN_SIZES)[:-1].tolist()
    a_q, a_k, a_v, b_q, b_k, b_v, z, xbc, dt_raw = jnp.split(h @ w_in, points, axis=-1)
    heads = lambda t, nh: t.reshape(b, n, nh, HEAD_DIM)
    a_q, a_k, a_v = heads(a_q, A_HEADS), heads(a_k, A_KV), heads(a_v, A_KV)
    b_q = rmsnorm(heads(b_q, B_HEADS), q_norm_g)
    b_k = rmsnorm(heads(b_k, B_KV), k_norm_g)
    b_v = heads(b_v, B_KV)
    if cache is None:
        o_a = attend_blocks(a_q, a_k, a_v, a_sink)
        o_b = attend_blocks(b_q, b_k, b_v, None)
        zeros = jnp.zeros((b, SSM_HEADS, SSM_HEAD_DIM, SSM_STATE), f32)
        o_c, h_f, h_b = mamba_mix(z, xbc, dt_raw, conv_w, conv_b, dt_bias, a_log, d_skip, ssm_norm_g,
                                  zeros, zeros)
        new = (a_k, a_v, b_k, b_v, h_f, h_b)
    else:
        ck_a, cv_a, ck_b, cv_b, h0_f, h0_b, cos, sin = cache
        a_q, a_k = apply_rope(a_q, cos, sin), apply_rope(a_k, cos, sin)
        b_q, b_k = apply_rope(b_q, cos, sin), apply_rope(b_k, cos, sin)
        o_a = banded_attention(a_q, a_k, a_v, ck_a.astype(a_k.dtype), cv_a.astype(a_v.dtype), a_sink)
        o_b = attend_blocks(b_q, jnp.concatenate([b_k, ck_b.astype(b_k.dtype)], axis=1),
                            jnp.concatenate([b_v, cv_b.astype(b_v.dtype)], axis=1), None)
        o_c, _, _ = mamba_mix(z, xbc, dt_raw, conv_w, conv_b, dt_bias, a_log, d_skip, ssm_norm_g,
                              h0_f, h0_b)
        new = None
    o = jnp.concatenate([o_a.reshape(b, n, -1), o_b.reshape(b, n, -1), o_c.astype(o_a.dtype)], axis=-1)
    return o @ w_out, new

def hier_moe(h, w_rg, b_rg, w_re, b_re, w_gate, w_up, w_down):
    shp = h.shape
    t = h.reshape(-1, shp[-1])
    n_tok = t.shape[0]
    tok = jnp.arange(n_tok)
    g_logit = (t @ w_rg + b_rg).astype(f32)
    g_prob = jax.nn.softmax(g_logit, axis=-1)
    g_sel = jnp.argmax(g_logit, axis=-1)
    e_logit = (t @ w_re + b_re).astype(f32).reshape(n_tok, N_EGROUPS, EXPERTS_PER_GROUP)
    e_in = e_logit[tok, g_sel]
    top_val, top_idx = lax.top_k(e_in, TOP_K_IN_GROUP)
    w_pair = jax.nn.softmax(top_val, axis=-1) * g_prob[tok, g_sel][:, None]
    expert = g_sel[:, None] * EXPERTS_PER_GROUP + top_idx
    combine = jnp.einsum('tk,tke->te', w_pair, jax.nn.one_hot(expert, N_EXPERTS, dtype=f32))
    hid = jax.nn.silu(jnp.einsum('td,edf->tef', t, w_gate)) * jnp.einsum('td,edf->tef', t, w_up)
    y = jnp.einsum('tef,efd->td', hid * combine[..., None].astype(hid.dtype), w_down)
    return y.reshape(shp).astype(h.dtype)

def layer_step(x, mod, n1, n2, w_in, a_sink, q_norm_g, k_norm_g, conv_w, conv_b, dt_bias, a_log, d_skip,
               ssm_norm_g, w_out, w_rg, b_rg, w_re, b_re, w_gate, w_up, w_down, cache):
    sh1, sc1, g1, sh2, sc2, g2 = jnp.split(mod, 6, axis=-1)
    o, new = mix_layer(modulate(rmsnorm(x, n1), sh1, sc1), w_in, a_sink, q_norm_g, k_norm_g, conv_w, conv_b,
                       dt_bias, a_log, d_skip, ssm_norm_g, w_out, cache)
    x = x + g1 * o
    x = x + g2 * hier_moe(modulate(rmsnorm(x, n2), sh2, sc2), w_rg, b_rg, w_re, b_re, w_gate, w_up, w_down)
    return x, new

def setup_inputs(seed: int = 0) -> dict:
    key = jax.random.key(seed)
    ks = jax.random.split(key, 40)
    nrm = lambda k, shape, s: jax.random.normal(k, shape, f32) * s
    dt0 = jnp.exp(jax.random.uniform(ks[20], (DEPTH, 2, SSM_HEADS), f32, math.log(1e-3), math.log(1e-1)))
    return {
        'x_prompt': nrm(ks[0], (BATCH, SEQ, D_MODEL), 1.0),
        'x_sample': nrm(ks[1], (DEC_BATCH, DEC_SEQ, D_MODEL), 1.0),
        'cache_a_k': nrm(ks[2], (DEC_BATCH, DEPTH, PAST_LEN, A_KV, HEAD_DIM), 1.0),
        'cache_a_v': nrm(ks[3], (DEC_BATCH, DEPTH, PAST_LEN, A_KV, HEAD_DIM), 1.0),
        'cache_b_k': nrm(ks[4], (DEC_BATCH, DEPTH, PAST_LEN, B_KV, HEAD_DIM), 1.0),
        'cache_b_v': nrm(ks[5], (DEC_BATCH, DEPTH, PAST_LEN, B_KV, HEAD_DIM), 1.0),
        'state_ssm_fwd': nrm(ks[6], (DEC_BATCH, DEPTH, SSM_HEADS, SSM_HEAD_DIM, SSM_STATE), 0.1),
        'state_ssm_bwd': nrm(ks[7], (DEC_BATCH, DEPTH, SSM_HEADS, SSM_HEAD_DIM, SSM_STATE), 0.1),
        'c': nrm(ks[8], (DEC_BATCH, D_MODEL), 1.0),
        'c_ctx': nrm(ks[9], (D_MODEL,), 1.0),
        'norm1_g': 1.0 + nrm(ks[10], (DEPTH, D_MODEL), 0.02),
        'norm2_g': 1.0 + nrm(ks[11], (DEPTH, D_MODEL), 0.02),
        'final_norm_g': 1.0 + nrm(ks[12], (D_MODEL,), 0.02),
        'w_ada': nrm(ks[13], (DEPTH, D_MODEL, 6 * D_MODEL), 0.5 * D_MODEL ** -0.5),
        'b_ada': nrm(ks[14], (DEPTH, 6 * D_MODEL), 0.02),
        'w_in': nrm(ks[15], (DEPTH, D_MODEL, D_IN), D_MODEL ** -0.5),
        'a_sink': nrm(ks[16], (DEPTH, A_HEADS), 0.5),
        'q_norm_g': 1.0 + nrm(ks[17], (DEPTH, HEAD_DIM), 0.02),
        'k_norm_g': 1.0 + nrm(ks[18], (DEPTH, HEAD_DIM), 0.02),
        'conv_w': nrm(ks[19], (DEPTH, CONV_W, XBC_DIM), CONV_W ** -0.5),
        'conv_b': nrm(ks[21], (DEPTH, XBC_DIM), 0.02),
        'dt_bias': dt0 + jnp.log(-jnp.expm1(-dt0)),
        'a_log': jnp.log(jax.random.uniform(ks[22], (DEPTH, 2, SSM_HEADS), f32, 1.0, 16.0)),
        'd_skip': 1.0 + nrm(ks[23], (DEPTH, SSM_HEADS), 0.1),
        'ssm_norm_g': 1.0 + nrm(ks[24], (DEPTH, D_SSM), 0.02),
        'w_out': nrm(ks[25], (DEPTH, D_MIX, D_MODEL), D_MIX ** -0.5),
        'w_router_group': nrm(ks[26], (DEPTH, D_MODEL, N_EGROUPS), D_MODEL ** -0.5),
        'b_router_group': nrm(ks[27], (DEPTH, N_EGROUPS), 0.01),
        'w_router_expert': nrm(ks[28], (DEPTH, D_MODEL, N_EXPERTS), D_MODEL ** -0.5),
        'b_router_expert': nrm(ks[29], (DEPTH, N_EXPERTS), 0.01),
        'w_gate': nrm(ks[30], (DEPTH, N_EXPERTS, D_MODEL, D_EXPERT), D_MODEL ** -0.5),
        'w_up': nrm(ks[31], (DEPTH, N_EXPERTS, D_MODEL, D_EXPERT), D_MODEL ** -0.5),
        'w_down': nrm(ks[32], (DEPTH, N_EXPERTS, D_EXPERT, D_MODEL), D_EXPERT ** -0.5),
    }

def reference(x_prompt, x_sample, cache_a_k, cache_a_v, cache_b_k, cache_b_v, state_ssm_fwd, state_ssm_bwd,
              c, c_ctx, norm1_g, norm2_g, final_norm_g, w_ada, b_ada, w_in, a_sink, q_norm_g, k_norm_g,
              conv_w, conv_b, dt_bias, a_log, d_skip, ssm_norm_g, w_out, w_router_group, b_router_group,
              w_router_expert, b_router_expert, w_gate, w_up, w_down):
    n_rows = x_sample.shape[1] // GRID_W
    cos, sin = axial_rope_tables(n_rows)
    xp, xs = x_prompt, x_sample
    a_ks, a_vs, b_ks, b_vs, h_fs, h_bs = [], [], [], [], [], []
    for l in range(DEPTH):
        lw = (norm1_g[l], norm2_g[l], w_in[l], a_sink[l], q_norm_g[l], k_norm_g[l], conv_w[l], conv_b[l],
              dt_bias[l], a_log[l], d_skip[l], ssm_norm_g[l], w_out[l], w_router_group[l], b_router_group[l],
              w_router_expert[l], b_router_expert[l], w_gate[l], w_up[l], w_down[l])
        mod_ctx = (jax.nn.silu(c_ctx) @ w_ada[l] + b_ada[l])[None, None, :]
        xp, new = layer_step(xp, mod_ctx, *lw, None)
        a_ks.append(new[0]); a_vs.append(new[1]); b_ks.append(new[2]); b_vs.append(new[3])
        h_fs.append(new[4]); h_bs.append(new[5])
        mod_lat = (jax.nn.silu(c) @ w_ada[l] + b_ada[l])[:, None, :]
        cache = (cache_a_k[:, l], cache_a_v[:, l], cache_b_k[:, l], cache_b_v[:, l],
                 state_ssm_fwd[:, l], state_ssm_bwd[:, l], cos, sin)
        xs, _ = layer_step(xs, mod_lat, *lw, cache)
    y_prompt = rmsnorm(xp, final_norm_g)
    y_sample = rmsnorm(xs, final_norm_g)
    new_a_k = jnp.stack(a_ks, axis=1)
    new_a_v = jnp.stack(a_vs, axis=1)
    new_b_k = jnp.stack(b_ks, axis=1)
    new_b_v = jnp.stack(b_vs, axis=1)
    new_ssm_fwd = jnp.stack(h_fs, axis=1)
    new_ssm_bwd = jnp.stack(h_bs, axis=1)
    return (y_prompt, y_sample, new_a_k, new_a_v, new_b_k, new_b_v, new_ssm_fwd, new_ssm_bwd)


_drawn_inputs = setup_inputs


def setup_inputs(seed=0):
    import zlib

    import numpy as np

    out = dict(_drawn_inputs(seed))
    spreads = {}
    factors = {'cache_a_k': 4.786,
     'cache_a_v': 4.043,
     'cache_b_k': 6.003,
     'cache_b_v': 4.856,
     'norm2_g': 3.205,
     'final_norm_g': 2.874,
     'a_sink': 8.0,
     'q_norm_g': 8.0,
     'k_norm_g': 3.009,
     'd_skip': 3.666,
     'ssm_norm_g': 8.0,
     'b_router_group': 8.0,
     'b_router_expert': 8.0}
    for name, (base, spread) in spreads.items():
        noise = np.random.default_rng([zlib.crc32(name.encode()), seed]).standard_normal(out[name].shape)
        drawn = base * np.exp(spread * noise) if base else spread * noise
        out[name] = __import__('jax').numpy.asarray(drawn.astype(out[name].dtype))
    for name, factor in factors.items():
        out[name] = (out[name] * factor).astype(out[name].dtype)
    return out
```

```python
from contextlib import ExitStack

import numpy as np

import concourse.bass as bass
from concourse import mybir
from concourse.alu_op_type import AluOpType as ALU

ACT = mybir.ActivationFunctionType
F32 = mybir.dt.float32
F32R = mybir.dt.float32r
BF16 = mybir.dt.bfloat16
I32 = mybir.dt.int32
AX = mybir.AxisListType

P = 128
DEPTH, D, SEQ, DEC = 2, 1024, 128, 256
KD = D // P
TILES = (SEQ + DEC) // P
TOK = TILES * P
HD = 64
NH, NKV = 4, 2
SH, SG, DS = 8, 2, 512
XBC, DT = 768, 16
D_IN = 2320
OFF_B, OFF_Z, OFF_XBC, OFF_DT = 512, 1024, 1536, 2304
NG, EPG, FE = 4, 4, 256
NE = NG * EPG
EPS = 1e-6
SCALE = HD ** -0.5
BIG = 1e30
PIECE = 2048
RING = 8
ADA_THIRD = 16
WINDOW = 128
SH1, SC1, G1, SH2, SC2, G2 = (8 * i for i in range(6))

R_N1, R_N2, R_BADA, R_CW, R_CB, R_SG = 0, 8, 16, 64, 82, 88
N_PROW = 92
T_DTB, T_AL, T_DSK, T_SINK, T_BG, T_BE, T_GQK = 0, 16, 32, 40, 44, 48, 64
N_TAB = T_GQK + 6 * HD
names = ["ident", "incl_f", "incl_b", "after", "before", "ones", "iota"]
C_AT = {n: P * i for i, n in enumerate(names)}
C_MASK = P * len(names)
C_COS = C_MASK + 2 * DEC
C_SIN = C_COS + 2 * HD
N_CONST = C_SIN + 2 * HD


def constants():
    k, c = np.arange(P)[:, None], np.arange(P)[None, :]
    t = np.zeros((P, N_CONST), np.float32)
    for n, v in (("ident", k == c), ("incl_f", k <= c), ("incl_b", k >= c), ("after", k > c),
                 ("before", k < c), ("ones", k == k + 0 * c), ("iota", c + 0 * k)):
        t[:, C_AT[n]:C_AT[n] + P] = v
    key = np.arange(DEC)[None, :]
    for b in range(2):
        t[:, C_MASK + DEC * b:C_MASK + DEC * (b + 1)] = np.where(np.abs(key - (b * P + k)) <= WINDOW, 0.0, -BIG)
    quarter = HD // 4
    inv = (10000.0 ** (-np.arange(quarter, dtype=np.float32) / quarter)).astype(np.float32)
    for b in range(2):
        pos = b * P + np.arange(P)
        r, w = (pos // 64).astype(np.float32)[:, None] * inv, (pos % 64).astype(np.float32)[:, None] * inv
        ang = np.concatenate([r, r, w, w], 1)
        sign = np.repeat(np.array([-1, 1, -1, 1], np.float32), quarter)
        t[:, C_COS + HD * b:C_COS + HD * (b + 1)] = np.cos(ang)
        t[:, C_SIN + HD * b:C_SIN + HD * (b + 1)] = np.sin(ang) * sign
    return t


HEADS = [(m, t, h) for m in (1, 2, 0) for t in range(2) for h in range(NH)]


def head_steps():
    n = len(HEADS)
    out = []
    for u in range(n + 3):
        if u < n:
            out.append(("scores", u))
        if 2 <= u < n + 2:
            out.append(("turn", u - 2))
        if u >= 3:
            out.append(("values", u - 3))
    return out


def layer_steps(l, passes):
    ada = [("ada", l, t, k) for t in (1, 2) for k in range(KD)]
    if l + 1 < DEPTH:
        ada += [("ada", l + 1, 0, k) for k in range(KD)]
    s = [("norm", 0), ("xbc",), ("rows", 0), ("ssm_in", 0), ("prep", 0), ("seg", 0), ("rows", 1), ("ssm_y", 0),
         ("ssm_in", 1), ("turn_qk", 0), ("seg", 1), ("prep", 1), ("rows_last",), ("ssm_y", 1), ("ssm_in", 2),
         ("turn_qk", 1), ("prep", 2), ("seg", 2), ("silu_z",)]
    s += ada[:1] + [("ssm_y", 2)] + ada[1:2] + [("turn_qk", 2)] + [("ssm_off", 1), ("ssm_off", 2)]
    heads = head_steps()
    rest = ada[2:]
    done = 0
    for i, h in enumerate(heads):
        s.append(h)
        want = len(rest) * (i + 1) // len(heads)
        s += rest[done:want]
        done = want
    s += [("gate",), ("turn_mix",), ("wout",), ("norm", 1), ("router",), ("hrow",), ("rank",)]
    for p in range(passes):
        s += [("select", p), ("gather", p)]
        for e in range(NE):
            s.append(("gu", p, e))
            if e:
                s.append(("down", p, e - 1))
        s += [("down", p, NE - 1), ("scatter", p)]
    return s


def build(nc, a, a_out):
    PASSES = TILES
    pieces = [("ada", 0, 0, k) for k in range(KD)]
    STEPS = [layer_steps(l, PASSES) for l in range(DEPTH)]
    for l in range(DEPTH):
        for s in STEPS[l]:
            if s[0] == "xbc":
                pieces += [("xbc", l, i) for i in range(KD // 2)] + [("win", l, k) for k in range(KD)]
            elif s[0] == "ada":
                pieces.append(s)
            elif s[0] == "wout":
                pieces += [("wout", l, i) for i in range(KD // 2)]
            elif s[0] == "gu":
                pieces += [("gate", l, *s[1:]), ("up", l, *s[1:])]
            elif s[0] == "down":
                pieces.append(("down", l, *s[1:]))
    piece_at = {key: n for n, key in enumerate(pieces)}
    assert len(piece_at) == len(pieces)

    with ExitStack() as ctx:
        def sb(name, shape, dt=F32, c=ctx):
            return c.enter_context(nc.sbuf_tensor(name, shape, dt))[:]

        all_sems = {}

        def sem(name):
            all_sems[name] = ctx.enter_context(nc.semaphore(name))
            return all_sems[name]

        def counter():
            n = [0]

            def more():
                n[0] += 1
                return n[0]
            return more

        xT = sb("xT", [P, KD, TOK])
        hT = sb("hT", [P, KD, TOK])
        ring = sb("ring", [P, RING, PIECE])
        const = sb("const", [P, N_CONST])
        prow = sb("prow", [P, 3, P])
        pcol = sb("pcol", [P, 2 * N_PROW + 24])
        tab = sb("tab", [P, DEPTH, N_TAB])
        silu_c = sb("silu_c", [P, KD, 2])
        mods = sb("mods", [P, DEPTH, 48, 2])
        amul = sb("amul", [P, DEPTH, 2, KD, 2])
        eps_col = sb("eps_col", [P, 1])
        one_col = sb("one_col", [P, 1])
        lnrow = sb("lnrow", [P, TOK])
        ident_b = sb("ident_b", [P, P], BF16)
        mask_b = sb("mask_b", [P, 2, DEC], BF16)
        nsink = sb("nsink", [P, DEPTH, NH])
        a_exp = sb("a_exp", [P, DEPTH, DT])
        ctx_rows = sb("ctx_rows", [P, DEPTH, 4, NKV * HD])
        ckT = sb("ckT", [P, DEPTH, 2, P])
        h0 = hT.rearrange("p c t -> p (c t)")[:, 0:DEPTH * 512].rearrange("p (l d j g n) -> p l d j g n", l=DEPTH, d=2, j=2, g=2)
        h0T = sb("h0T", [P, DEPTH, 2, 2 * P])
        wr = sb("wr", [P, DEPTH, KD, NG + NE])
        small = sb("small", [P, 32])

        def c_(name, n=P):
            return const[:, C_AT[name]:C_AT[name] + n]

        mix = ExitStack()
        with mix:
            row = sb("row", [P, TILES, 1024], c=mix)
            z = sb("z", [P, TILES, DS], c=mix)
            xbc = sb("xbc", [P, 6, TOK], c=mix)
            qkT = sb("qkT", [P, 6, TOK], c=mix)
            pT = sb("pT", [P, 3, 3 * P], c=mix)
            y = sb("y", [P, TILES, DS], c=mix)
            xs = sb("xs", [P, DS], c=mix)
            bro = sb("bro", [P, P], c=mix)
            gm = sb("gm", [P, 2, 2, P], c=mix)
            xd = sb("xd", [P, 2, SH, HD], c=mix)
            xdd = sb("xdd", [P, 2, SH, HD], c=mix)
            ud = sb("ud", [P, 2, SH, P], c=mix)
            mm = sb("mm", [P, 2, SH, P], c=mix)
            hin = sb("hin", [P, 2, 2 * P], c=mix)
            tmp = sb("tmp", [P, 3, DS], c=mix)
            stout = sb("stout", [P, 2, 4, HD], c=mix)
            dts = sb("dts", [P, TILES, DT], c=mix)
            dav = sb("dav", [P, TILES, DT], c=mix)
            dtw = sb("dtw", [P, 6, TILES * DT], c=mix)
            ex = sb("ex", [P, TILES, 48], c=mix)
            att = sb("att", [P, 6, len(HEADS)], c=mix)
            nrm = sb("nrm", [P, 32], c=mix)
            probs = hT.rearrange("p c t -> p (c t)")[:, 0:4 * TOK].rearrange("p (b t) -> p b t", b=4)
            yx = sb("yx", [P, DS], c=mix)
            sq = row.rearrange("p m n -> p (m n)").rearrange("p (c t) -> p c t", c=KD)
        moe = ExitStack()
        with moe:
            h_hi = sb("h_hi", [P, TILES, KD, P], F32R, c=moe)
            h_lo = sb("h_lo", [P, TILES, KD, P], F32R, c=moe)
            sel = sb("sel", [P, TILES, NG, P], F32R, c=moe)
            selT = sb("selT", [P, NG, TOK], F32R, c=moe)
            xg = sb("xg", [P, KD, NG, P], c=moe)
            sg = sb("sg", [P, 2, FE], c=moe)
            hid = sb("hid", [P, 2, FE], c=moe)
            hidT = sb("hidT", [P, 2, FE], c=moe)
            y_hi = sb("y_hi", [P, NG, D], F32R, c=moe)
            y_lo = sb("y_lo", [P, NG, D], F32R, c=moe)
            lg = sb("lg", [P, TILES, NG + NE], c=moe)
            rt = sb("rt", [P, 24, TILES, NG], c=moe)
            e16 = sb("e16", [P, TILES, NE], c=moe)
            cwg = sb("cwg", [P, NG, EPG], c=moe)
        psum = ctx.enter_context(nc.psum_tensor("psum", [P, 8, 512], F32))[:]

        bank_full = [sem(f"bank{b}_full") for b in range(8)]
        bank_read = [sem(f"bank{b}_read") for b in range(8)]
        ring_full = [sem(f"ring{b}_full") for b in range(RING)]
        pieces_used = sem("pieces_used")
        const_in, x_in, prow_in, tab_in, cache_in, wr_in = (sem(n) for n in (
            "const_in", "x_in", "prow_in", "tab_in", "cache_in", "wr_in"))
        dve_step, act_step, pool_step = (sem(n) for n in ("dve_step", "act_step", "pool_step"))
        out_sem = [sem(f"out{i}") for i in range(6)]
        y_out = sem("y_out")
        cols_ready, siluc_ready = sem("cols_ready"), sem("siluc_ready")
        setup_act, setup_dve = sem("setup_act"), sem("setup_dve")
        sig, per = {}, {}
        dve_steps, act_steps, pool_steps = counter(), counter(), counter()
        for name, n in (
                ("sq", 8), ("rstd", 2), ("h", 16), ("xbc_silu", 6), ("dt_na", 1), ("dt_u", 1),
                ("dt_r", 1), ("da", 1), ("bss", 3), ("brs", 3), ("prep", 3), ("ud", 3), ("xd", 3), ("yx", 3),
                ("seg", 12), ("zs", 1), ("nb", 24), ("es", 12), ("yz", 1), ("yrs", 1), ("yn", 1),
                ("ge0", 1), ("ge", 1), ("ed0", 1), ("ed", 1), ("goh", 1), ("cw", 1), ("hhi", 6),
                ("sel", PASSES), ("sgl", NE * PASSES), ("yhi", 8 * PASSES)):
            sig[name], per[name] = sem(name), n

        block = ctx.enter_context(nc.Block())

        uses, read_at, fills, reads = {}, {}, [0] * 8, [0] * 8
        turn = [0]
        release, used_count = {}, [0]

        release, used_count = {}, counter()

        def fill(key, b=None):
            if b is None:
                turn[0] = (turn[0] + 1) % 7
                b = turn[0]
            before = reads[b]
            reads[b] += 1
            fills[b] += 1
            uses[key], read_at[key] = (b, fills[b]), reads[b]
            return bank_read[b], before

        def bank(key):
            return psum[:, uses[key][0], :]

        def filled(key):
            return bank_full[uses[key][0]], 1

        def full(key):
            return bank_full[uses[key][0]], uses[key][1]

        def was_read(key):
            return bank_read[uses[key][0]], 1

        def taken(key):
            return bank_read[uses[key][0]], read_at[key]

        def landed(key):
            n = piece_at[key]
            return ring_full[n % RING], 16 * (n // RING + 1)

        def slot(key):
            return ring[:, piece_at[key] % RING, :]

        def used(key):
            release[key] = (pieces_used, used_count())
            return pieces_used, 1

        def used_with(key, filling):
            release[key] = full(filling)

        def turn_probs(eng, copy, l, u):
            w = P if HEADS[u][0] == 0 else TOK
            key = ("turn", l, u)
            eng.wait_ge(*full(key))
            src = bank(key)
            if u >= 3:
                eng.wait_ge(*full(("values", l, u - 3)))
            copy(pT[:, u % 3, 0:w], src[:, 0:w]).then_inc(*was_read(key))

        def gathered(eng, copy, l, p, t):
            key = ("xg", l, p, t)
            eng.wait_ge(*full(key))
            src = bank(key)
            if p:
                eng.wait_ge(*full(("gu", l, p - 1, NE - 1)))
            copy(xg[:, t, :, :].rearrange("p g s -> p (g s)"), src).then_inc(*was_read(key))

        @block.tensor
        def _(pe):
            ident = c_("ident")

            def ada(l, t, k):
                key = ("ada", l, t)
                pe.wait_ge(*landed(("ada", l, t, k)))
                w = slot(("ada", l, t, k))
                if k == 0:
                    pe.wait_ge(*fill(key, 7))
                dst = psum[:, 7, :]
                for j in range(ADA_THIRD):
                    last = pe.matmul(dst[:, 2 * j:2 * j + 2], w[:, j * P:(j + 1) * P], silu_c[:, k, :],
                                     start=(k == 0 and j == 0), stop=(k == KD - 1), skip_group_check=True)
                if k == KD - 1:
                    last.then_inc(*filled(key))
                    used_with(("ada", l, t, k), key)
                else:
                    last.then_inc(*used(("ada", l, t, k)))

            pe.wait_ge(const_in, 16)
            pe.wait_ge(x_in, 32)
            for c in range(KD):
                pe.wait_ge(*fill(("xin", c)))
                dst = bank(("xin", c))
                for m in range(TILES):
                    last = pe.transpose(dst[:, m * P:(m + 1) * P], row[:, m, c * P:(c + 1) * P], ident)
                last.then_inc(*filled(("xin", c)))
            pe.wait_ge(prow_in, 16 * (6 * DEPTH + 3))
            pe.wait_ge(*fill(("pcol",)))
            dst = bank(("pcol",))
            for i, n in enumerate((N_PROW, N_PROW, 24)):
                last = pe.transpose(dst[:, i * N_PROW:i * N_PROW + n], prow[0:n, i, :], ident[0:n, 0:n])
            last.then_inc(*filled(("pcol",)))
            pe.wait_ge(cache_in, 16 * 12 * DEPTH)
            for l in range(DEPTH):
                pe.wait_ge(*fill(("ck", l)))
                dst = bank(("ck", l))
                for t in range(2):
                    last = pe.transpose(dst[:, t * P:(t + 1) * P], ctx_rows[:, l, t, :], ident)
                last.then_inc(*filled(("ck", l)))
                pe.wait_ge(*fill(("h0", l)))
                dst = bank(("h0", l))
                for d in range(2):
                    for j in range(2):
                        last = pe.transpose(dst[:, d * 256 + j * P:d * 256 + (j + 1) * P],
                                            h0[:, l, d, j, :, :].rearrange("p g n -> p (g n)"), ident)
                last.then_inc(*filled(("h0", l)))
            pe.wait_ge(siluc_ready, 1)
            pe.wait_ge(setup_dve, 1)
            pe.wait_ge(wr_in, 16 * 2 * DEPTH)
            for k in range(KD):
                ada(0, 0, k)

            def sums(key, l, n, base):
                pe.wait_ge(*fill(key))
                dst = bank(key)
                for c in range(KD):
                    if c % 2 == 0:
                        pe.wait_ge(sig["sq"], base + c // 2 + 1)
                    last = pe.matmul(dst[:, 0:TOK], c_("ones"), sq[:, c, :], start=(c == 0), stop=(c == KD - 1))
                last.then_inc(*filled(key))

            for l in range(DEPTH):
                for step in STEPS[l]:
                    kind, arg = step[0], step[1:]
                    if kind == "norm":
                        n = arg[0]
                        sums(("ss", l, n), l, n, (2 * l + n) * 4)
                    elif kind == "ada":
                        ada(*arg)
                    elif kind == "xbc":
                        for c in range(6):
                            pe.wait_ge(*fill(("xbc", l, c)))
                        dsts = [bank(("xbc", l, c)) for c in range(6)]
                        pe.wait_ge(*fill(("dt", l)))
                        dtd = bank(("dt", l))
                        for i in range(KD // 2):
                            pe.wait_ge(*landed(("xbc", l, i)))
                            w = slot(("xbc", l, i))[:, 0:2 * (XBC + DT)].rearrange("p (k n) -> p k n", k=2)
                            for kk in range(2):
                                k = 2 * i + kk
                                pe.wait_ge(sig["h"], per["h"] * l + k + 1)
                                for m in range(TILES):
                                    last = pe.matmul(dtd[:, m * DT:(m + 1) * DT], hT[:, k, m * P:(m + 1) * P],
                                                     w[:, kk, XBC:XBC + DT], start=(k == 0 and m == 0),
                                                     stop=(k == KD - 1), skip_group_check=True)
                                if k == KD - 1:
                                    last.then_inc(*filled(("dt", l)))
                                for c in range(6):
                                    last = pe.matmul(dsts[c][:, 0:TOK], w[:, kk, c * P:(c + 1) * P], hT[:, k, :],
                                                     start=(k == 0), stop=(k == KD - 1))
                                    if k == KD - 1:
                                        last.then_inc(*filled(("xbc", l, c)))
                            if i < KD // 2 - 1:
                                last.then_inc(*used(("xbc", l, i)))
                            else:
                                used_with(("xbc", l, i), ("xbc", l, 5))
                    elif kind == "rows":
                        m = arg[0]
                        for g in range(3):
                            pe.wait_ge(*fill(("row", l, m, g)))
                            dst = bank(("row", l, m, g))
                            for k in range(KD):
                                pe.wait_ge(*landed(("win", l, k)))
                                w = slot(("win", l, k))
                                last = pe.matmul(dst[:, 0:512], hT[:, k, m * P:(m + 1) * P],
                                                 w[:, g * 512:(g + 1) * 512], start=(k == 0), stop=(k == KD - 1))
                            last.then_inc(*filled(("row", l, m, g)))
                    elif kind == "rows_last":
                        m = TILES - 1
                        for g in range(3):
                            pe.wait_ge(*fill(("row", l, m, g)))
                        dsts = [bank(("row", l, m, g)) for g in range(3)]
                        for k in range(KD):
                            pe.wait_ge(*landed(("win", l, k)))
                            w = slot(("win", l, k))
                            for g in range(3):
                                last = pe.matmul(dsts[g][:, 0:512], hT[:, k, m * P:(m + 1) * P],
                                                 w[:, g * 512:(g + 1) * 512], start=(k == 0), stop=(k == KD - 1))
                                if k == KD - 1:
                                    last.then_inc(*filled(("row", l, m, g)))
                            if k < KD - 1:
                                last.then_inc(*used(("win", l, k)))
                            else:
                                used_with(("win", l, k), ("row", l, m, 2))
                    elif kind == "turn_qk":
                        m = arg[0]
                        pe.wait_ge(sig["prep"], per["prep"] * l + m + 1)
                        pe.wait_ge(*taken(("row", l, m, 0)))
                        pe.wait_ge(*taken(("row", l, m, 1)))
                        for t in range(2):
                            pe.wait_ge(*fill(("qkT", l, m, t)))
                            dst = bank(("qkT", l, m, t))
                            for i in range(3):
                                at = t * OFF_B + i * P
                                last = pe.transpose(dst[:, i * P:(i + 1) * P], row[:, m, at:at + P], ident)
                            last.then_inc(*filled(("qkT", l, m, t)))
                    elif kind == "ssm_in":
                        m = arg[0]
                        tok = slice(m * P, (m + 1) * P)
                        pe.wait_ge(sig["xbc_silu"], per["xbc_silu"] * l + 6)
                        pe.wait_ge(*fill(("xs", l, m)))
                        dst = bank(("xs", l, m))
                        for c in range(4):
                            last = pe.transpose(dst[:, c * P:(c + 1) * P], xbc[:, c, tok], ident)
                        last.then_inc(*filled(("xs", l, m)))
                        pe.wait_ge(*fill(("bg", l, m)))
                        dst = bank(("bg", l, m))
                        pe.transpose(dst[:, 0:P], xbc[:, 4, tok], ident)
                        for g in range(2):
                            if g:
                                pe.wait_ge(*fill(("bg1", l, m)))
                                dst = bank(("bg1", l, m))
                            last = pe.matmul(dst[:, P:2 * P], xbc[g * 64:g * 64 + 64, 4, tok],
                                             xbc[g * 64:g * 64 + 64, 5, tok], start=True, stop=True)
                            last.then_inc(*filled(("bg1" if g else "bg", l, m)))
                        pe.wait_ge(sig["da"], per["da"] * l + 1)
                        pe.wait_ge(*fill(("cum", l, m)))
                        dst = bank(("cum", l, m))
                        for i, (tri_f, tri_b) in enumerate((("incl_f", "incl_b"), ("after", "before"))):
                            pe.matmul(dst[:, 16 * i:16 * i + 8], c_(tri_f), dav[:, m, 0:8], start=True, stop=True)
                            pe.matmul(dst[:, 16 * i + 8:16 * i + 16], c_(tri_b), dav[:, m, 8:16], start=True, stop=True)
                        last = pe.matmul(dst[:, 32:48], c_("ones"), dav[:, m, :], start=True, stop=True)
                        last.then_inc(*filled(("cum", l, m)))
                    elif kind == "seg":
                        m = arg[0]
                        pe.wait_ge(sig["ud"], per["ud"] * l + m + 1)
                        for d, tri in enumerate(("after", "before")):
                            for g in range(2):
                                pe.wait_ge(*fill(("seg", l, m, d, g)))
                                dst = bank(("seg", l, m, d, g))
                                last = pe.matmul(dst[:, 0:512], c_(tri),
                                                 ud[:, d, 4 * g:4 * g + 4, :].rearrange("p h t -> p (h t)"),
                                                 start=True, stop=True)
                                last.then_inc(*filled(("seg", l, m, d, g)))
                    elif kind == "ssm_y":
                        m = arg[0]
                        for d in range(2):
                            for g in range(2):
                                pe.wait_ge(*taken(("seg", l, m, d, g)))
                        pe.wait_ge(*taken(("bg", l, m)))
                        pe.wait_ge(*taken(("bg1", l, m)))
                        pe.wait_ge(sig["xd"], per["xd"] * l + m + 1)
                        pe.wait_ge(*fill(("ydiag", l, m)))
                        dst = bank(("ydiag", l, m))
                        for h in range(SH):
                            for d in range(2):
                                last = pe.matmul(dst[:, h * HD:(h + 1) * HD], mm[:, d, h, :], xd[:, d, h, :],
                                                 start=(d == 0), stop=(d == 1))
                        last.then_inc(*filled(("ydiag", l, m)))
                        pe.wait_ge(*fill(("state", l, m)))
                        dst = bank(("state", l, m))
                        if m == 0:
                            for d in range(2):
                                for pr in range(4):
                                    g = pr // 2
                                    last = pe.matmul(dst[:, d * 256 + pr * HD:d * 256 + (pr + 1) * HD],
                                                     xdd[:, d, 2 * pr:2 * pr + 2, :].rearrange("p h n -> p (h n)"),
                                                     bro[:, g * 64:g * 64 + 64], start=True, stop=True)
                        else:
                            d = m - 1
                            for g in range(2):
                                last = pe.matmul(dst[g * 64:g * 64 + 64, 0:256], bro[:, g * 64:g * 64 + 64],
                                                 xdd[:, d, 4 * g:4 * g + 4, :].rearrange("p h n -> p (h n)"),
                                                 start=True, stop=True)
                        last.then_inc(*filled(("state", l, m)))
                    elif kind == "ssm_off":
                        m = arg[0]
                        pe.wait_ge(*taken(("state", l, 1)))
                        pe.wait_ge(*taken(("state", l, 2)))
                        for g in range(2):
                            pe.wait_ge(*fill(("yoff", l, m, g)))
                            dst = bank(("yoff", l, m, g))
                            for d in range(2):
                                src = h0T[:, l, d, :] if (m, d) in ((1, 0), (2, 1)) else hin[:, d, :]
                                last = pe.matmul(dst[:, d * 256:(d + 1) * 256],
                                                 xbc[g * 64:g * 64 + 64, 5, m * P:(m + 1) * P],
                                                 src[g * 64:g * 64 + 64, :], start=True, stop=True)
                            last.then_inc(*filled(("yoff", l, m, g)))
                    elif kind == "scores":
                        u = arg[0]
                        m, t, h = HEADS[u]
                        kv, i = h // 2, h % 2
                        part = slice(kv * 64, kv * 64 + 64)
                        if u == 0:
                            for mq in range(TILES):
                                for tq in range(2):
                                    pe.wait_ge(*taken(("qkT", l, mq, tq)))
                        pe.wait_ge(*fill(("scores", l, u)))
                        dst = bank(("scores", l, u))
                        q = qkT[part, 3 * t + i, m * P:(m + 1) * P]
                        if m == 0:
                            last = pe.matmul(dst[:, 0:P], q, qkT[part, 3 * t + 2, 0:P], start=True, stop=True)
                        else:
                            pe.matmul(dst[:, 0:DEC], q, qkT[part, 3 * t + 2, P:TOK], start=True, stop=(t == 1))
                            if t == 0:
                                pe.matmul(dst[:, 0:DEC], ident_b, mask_b[:, m - 1, :], start=False, stop=True)
                            last = pe.matmul(dst[:, DEC:DEC + P], q, ckT[part, l, t, :], start=True, stop=True)
                        last.then_inc(*filled(("scores", l, u)))
                    elif kind == "turn":
                        u = arg[0]
                        m = HEADS[u][0]
                        pe.wait_ge(*taken(("scores", l, u)))
                        pe.wait_ge(*fill(("turn", l, u)))
                        dst = bank(("turn", l, u))
                        for c in range(1 if m == 0 else 3):
                            last = pe.transpose(dst[:, c * P:(c + 1) * P], probs[:, u % 4, c * P:(c + 1) * P], ident)
                        last.then_inc(*filled(("turn", l, u)))
                    elif kind == "values":
                        u = arg[0]
                        m, t, h = HEADS[u]
                        v = slice(t * OFF_B + 384 + (h // 2) * HD, t * OFF_B + 384 + (h // 2) * HD + HD)
                        pe.wait_ge(*taken(("turn", l, u)))
                        pe.wait_ge(*fill(("values", l, u)))
                        dst = bank(("values", l, u))
                        srcs = [row[:, 0, v]] if m == 0 else [row[:, 1, v], row[:, 2, v],
                                                              ctx_rows[:, l, 2 + t, (h // 2) * HD:(h // 2) * HD + HD]]
                        for c, vv in enumerate(srcs):
                            last = pe.matmul(dst[:, 0:HD], pT[:, u % 3, c * P:(c + 1) * P], vv,
                                             start=(c == 0), stop=(c == len(srcs) - 1))
                        last.then_inc(*filled(("values", l, u)))
                    elif kind == "turn_mix":
                        for u in range(len(HEADS) - 7, len(HEADS)):
                            pe.wait_ge(*taken(("values", l, u)))
                        for c in range(KD):
                            if c == 4:
                                pe.wait_ge(sig["yn"], per["yn"] * l + 1)
                            pe.wait_ge(*fill(("mix", l, c)))
                            dst = bank(("mix", l, c))
                            for m in range(TILES):
                                src = row[:, m, (0, P, OFF_B, OFF_B + P)[c]:(0, P, OFF_B, OFF_B + P)[c] + P] if c < 4 \
                                    else y[:, m, (c - 4) * P:(c - 3) * P]
                                last = pe.transpose(dst[:, m * P:(m + 1) * P], src, ident)
                            last.then_inc(*filled(("mix", l, c)))
                    elif kind == "wout":
                        for c in range(KD):
                            pe.wait_ge(*fill(("wout", l, c)))
                            dst = bank(("wout", l, c))
                            for k in range(KD):
                                if c == 0:
                                    pe.wait_ge(*taken(("mix", l, k)))
                                pe.wait_ge(*landed(("wout", l, k // 2)))
                                w = slot(("wout", l, k // 2))
                                last = pe.matmul(dst[:, 0:TOK], w[:, (k % 2) * D + c * P:(k % 2) * D + (c + 1) * P],
                                                 hT[:, k, :], start=(k == 0), stop=(k == KD - 1))
                                if c == KD - 1 and k % 2 and k < KD - 1:
                                    last.then_inc(*used(("wout", l, k // 2)))
                            last.then_inc(*filled(("wout", l, c)))
                        used_with(("wout", l, 3), ("wout", l, KD - 1))
                    elif kind == "router":
                        pe.wait_ge(sig["h"], per["h"] * l + 16)
                        pe.wait_ge(*fill(("logits", l)))
                        dst = bank(("logits", l))
                        n = NG + NE
                        for m in range(TILES):
                            for k in range(KD):
                                last = pe.matmul(dst[:, m * n:(m + 1) * n], hT[:, k, m * P:(m + 1) * P], wr[:, l, k, :],
                                                 start=(k == 0), stop=(k == KD - 1))
                        last.then_inc(*filled(("logits", l)))
                    elif kind == "hrow":
                        for m in range(TILES):
                            for half in range(2):
                                pe.wait_ge(*fill(("hrow", l, m, half)))
                                dst = bank(("hrow", l, m, half))
                                for j in range(4):
                                    last = pe.transpose(dst[:, j * P:(j + 1) * P],
                                                        hT[:, 4 * half + j, m * P:(m + 1) * P], ident)
                                last.then_inc(*filled(("hrow", l, m, half)))
                    elif kind == "rank":
                        pe.wait_ge(sig["goh"], per["goh"] * l + 1)
                        pe.wait_ge(*fill(("rank", l)))
                        dst = bank(("rank", l))
                        for m in range(TILES):
                            for mm_ in range(m + 1):
                                last = pe.matmul(dst[:, m * NG:(m + 1) * NG], c_("before" if mm_ == m else "ones"),
                                                 rt[:, 0, mm_, :], start=(mm_ == 0), stop=(mm_ == m))
                        last.then_inc(*filled(("rank", l)))
                    elif kind == "select":
                        p = arg[0]
                        pe.wait_ge(sig["sel"], per["sel"] * l + p + 1)
                        for g in range(NG):
                            pe.wait_ge(*fill(("selT", l, p, g)))
                            dst = bank(("selT", l, p, g))
                            for m in range(TILES):
                                last = pe.transpose(dst[:, m * P:(m + 1) * P], sel[:, m, g, :].bitcast(F32), ident)
                            last.then_inc(*filled(("selT", l, p, g)))
                        pe.wait_ge(sig["cw"], per["cw"] * l + 1)
                        pe.wait_ge(*fill(("cwg", l, p)))
                        dst = bank(("cwg", l, p))
                        for g in range(NG):
                            for m in range(TILES):
                                last = pe.matmul(dst[:, g * EPG:(g + 1) * EPG], sel[:, m, g, :].bitcast(F32),
                                                 rt[:, 1, m, :], start=(m == 0), stop=(m == TILES - 1))
                        last.then_inc(*filled(("cwg", l, p)))
                    elif kind == "gather":
                        p = arg[0]
                        for m in range(TILES):
                            for half in range(2):
                                pe.wait_ge(*taken(("hrow", l, m, half)))
                        for t in range(KD):
                            pe.wait_ge(*fill(("xg", l, p, t)))
                            dst = bank(("xg", l, p, t))
                            for i, src in enumerate((h_hi, h_lo)):
                                for m in range(TILES):
                                    last = pe.matmul(dst[:, 0:NG * P], src[:, m, t, :],
                                                     sel[:, m, :, :].rearrange("p g s -> p (g s)"),
                                                     start=(i == 0 and m == 0), stop=(i == 1 and m == TILES - 1))
                            last.then_inc(*filled(("xg", l, p, t)))
                    elif kind == "gu":
                        p, e = arg
                        g = e // EPG
                        if e == 0:
                            for t in range(KD):
                                pe.wait_ge(*taken(("xg", l, p, t)))
                        for i, name in enumerate(("gate", "up")):
                            pe.wait_ge(*landed((name, l, p, e)))
                            w = slot((name, l, p, e)).rearrange("p (t f) -> p t f", t=KD)
                            if i == 0:
                                pe.wait_ge(*fill(("gu", l, p, e), 4 + e % 2))
                                dst = bank(("gu", l, p, e))
                            for t in range(KD):
                                last = pe.matmul(dst[:, i * FE:(i + 1) * FE], xg[:, t, g, :], w[:, t, :],
                                                 start=(t == 0), stop=(t == KD - 1))
                            if i == 0:
                                last.then_inc(*used((name, l, p, e)))
                            else:
                                last.then_inc(*filled(("gu", l, p, e)))
                                used_with((name, l, p, e), ("gu", l, p, e))
                    elif kind == "down":
                        p, e = arg
                        g = e // EPG
                        pe.wait_ge(*taken(("gu", l, p, e)))
                        pe.wait_ge(*fill(("hidT", l, p, e), 6))
                        dst = bank(("hidT", l, p, e))
                        for f in range(2):
                            last = pe.transpose(dst[:, f * P:(f + 1) * P], hid[:, e % 2, f * P:(f + 1) * P], ident)
                        last.then_inc(*filled(("hidT", l, p, e)))
                        pe.wait_ge(*taken(("hidT", l, p, e)))
                        pe.wait_ge(*landed(("down", l, p, e)))
                        w = slot(("down", l, p, e)).rearrange("p (f n) -> p f n", f=2)
                        for half in range(2):
                            b = 2 * (g % 2) + half
                            if e % EPG == 0:
                                pe.wait_ge(*fill(("yg", l, p, g, half), b))
                            for f in range(2):
                                last = pe.matmul(psum[:, b, :], hidT[:, e % 2, f * P:(f + 1) * P],
                                                 w[:, f, half * 512:(half + 1) * 512],
                                                 start=(e % EPG == 0 and f == 0), stop=(e % EPG == EPG - 1 and f == 1))
                            if e % EPG == EPG - 1:
                                last.then_inc(*filled(("yg", l, p, g, half)))
                        if e % EPG == EPG - 1:
                            used_with(("down", l, p, e), ("yg", l, p, g, 1))
                        else:
                            last.then_inc(*used(("down", l, p, e)))
                    elif kind == "scatter":
                        p = arg[0]
                        for g in range(NG):
                            pe.wait_ge(*taken(("selT", l, p, g)))
                            for half in range(2):
                                pe.wait_ge(*taken(("yg", l, p, g, half)))
                        for c in range(KD):
                            pe.wait_ge(*fill(("sc", l, p, c)))
                            dst = bank(("sc", l, p, c))
                            for i, src in enumerate((y_hi, y_lo)):
                                for g in range(NG):
                                    last = pe.matmul(dst[:, 0:TOK], src[:, g, c * P:(c + 1) * P], selT[:, g, :],
                                                     start=(i == 0 and g == 0), stop=(i == 1 and g == NG - 1))
                            last.then_inc(*filled(("sc", l, p, c)))
            sums(("ss", DEPTH, 0), DEPTH, 0, 2 * DEPTH * 4)
            for m in range(TILES):
                for half in range(2):
                    if m == 0 and half == 0:
                        pe.wait_ge(sig["h"], 16 * DEPTH + 8)
                    pe.wait_ge(*fill(("out", m, half)))
                    dst = bank(("out", m, half))
                    for j in range(4):
                        last = pe.transpose(dst[:, j * P:(j + 1) * P], hT[:, 4 * half + j, m * P:(m + 1) * P], ident)
                    last.then_inc(*filled(("out", m, half)))

        @block.sync
        def _(sp):
            sp.dma_start(const, a["const"]).then_inc(const_in, 16)
            sp.dma_start(row[:, 0, :], a["x_prompt"][0]).then_inc(x_in, 16)
            sp.dma_start(row[:, 1:3, :], a["x_sample"][0].rearrange("(m p) d -> p m d", p=P)).then_inc(x_in, 16)
            for n, key in enumerate(pieces):
                if n >= RING:
                    sp.wait_ge(*release[pieces[n - RING]])
                slot = ring[:, n % RING, :]
                kind, l, at = key[0], key[1], key[2:]
                if kind == "ada":
                    t, k = at
                    src, dst = a["w_ada"][l, k * P:(k + 1) * P, t * PIECE:(t + 1) * PIECE], slot
                elif kind == "xbc":
                    src = a["w_in"][l, 2 * at[0] * P:2 * (at[0] + 1) * P, OFF_XBC:D_IN].rearrange(
                        "(k p) n -> p k n", p=P)
                    dst = slot[:, 0:2 * (XBC + DT)].rearrange("p (k n) -> p k n", k=2)
                elif kind == "win":
                    src, dst = a["w_in"][l, at[0] * P:(at[0] + 1) * P, 0:OFF_XBC], slot[:, 0:OFF_XBC]
                elif kind == "wout":
                    src = a["w_out"][l, 2 * at[0] * P:2 * (at[0] + 1) * P, :].rearrange("(k p) n -> p k n", p=P)
                    dst = slot.rearrange("p (k n) -> p k n", k=2)
                elif kind == "down":
                    src = a["w_down"][l, at[1]].rearrange("(f p) n -> p f n", p=P)
                    dst = slot.rearrange("p (f n) -> p f n", f=2)
                else:
                    src = a["w_" + kind][l, at[1]].rearrange("(p t) f -> p (t f)", t=KD)
                    dst = slot
                sp.dma_start(dst, src).then_inc(ring_full[n % RING], 16)
            for m in range(TILES):
                for half in range(2):
                    sp.wait_ge(*taken(("out", m, half)))
                dst = a_out[0][0] if m == 0 else a_out[1][0, (m - 1) * P:m * P, :]
                sp.dma_start(dst, row[:, m, :]).then_inc(y_out, 16)
            sp.wait_ge(y_out, 16 * TILES)
            for s in out_sem:
                sp.wait_ge(s, 16 * DEPTH)

        @block.scalar
        def _(act):

            for l in range(DEPTH):
                for name, r, n in (("norm1_g", R_N1, 8), ("norm2_g", R_N2, 8), ("b_ada", R_BADA, 48),
                                   ("conv_b", R_CB, 6), ("ssm_norm_g", R_SG, 4)):
                    act.dma_start(prow[r:r + n, l, :], a[name][l].rearrange("(r p) -> r p", p=P)).then_inc(prow_in, 16)
                act.dma_start(prow[R_CW:R_CW + 18, l, :],
                              a["conv_w"][l].rearrange("t (r p) -> (t r) p", p=P)).then_inc(prow_in, 16)
            for i, src in enumerate((a["final_norm_g"], a["c_ctx"], a["c"][0])):
                act.dma_start(prow[8 * i:8 * i + 8, 2, :], src.rearrange("(r p) -> r p", p=P)).then_inc(prow_in, 16)
            for l in range(DEPTH):
                for name, at, n in (("dt_bias", T_DTB, 16), ("a_log", T_AL, 16), ("d_skip", T_DSK, 8),
                                    ("a_sink", T_SINK, 4), ("b_router_group", T_BG, 4), ("b_router_expert", T_BE, 16)):
                    src = a[name][l]
                    if len(src.shape) == 2:
                        src = src.rearrange("a b -> (a b)")
                    act.dma_start(tab[:, l, at:at + n], src.partition_broadcast(P)).then_inc(tab_in, 16)
                for name, at, n in (("q_norm_g", T_GQK, 4), ("k_norm_g", T_GQK + 4 * HD, 2)):
                    act.dma_start(tab[:, l, at:at + n * HD].rearrange("p (a b) -> p a b", a=n),
                                  a[name][l].unsqueeze(0).unsqueeze(0).to_broadcast((P, n, HD))).then_inc(tab_in, 16)
                for i, name in enumerate(("cache_a_k", "cache_b_k", "cache_a_v", "cache_b_v")):
                    act.dma_start(ctx_rows[:, l, i, :], a[name][0, l].rearrange("s k d -> s (k d)"))\
                        .then_inc(cache_in, 16)
                for d, name in enumerate(("state_ssm_fwd", "state_ssm_bwd")):
                    for j in range(2):
                        for g in range(2):
                            act.dma_start(h0[:, l, d, j, g, :],
                                          a[name][0, l, 4 * g + 2 * j:4 * g + 2 * j + 2].rearrange("h p n -> (h p) n"))\
                                .then_inc(cache_in, 16)
                act.dma_start(wr[:, l, :, 0:NG], a["w_router_group"][l].rearrange("(k p) n -> p k n", p=P))\
                    .then_inc(wr_in, 16)
                act.dma_start(wr[:, l, :, NG:], a["w_router_expert"][l].rearrange("(k p) n -> p k n", p=P))\
                    .then_inc(wr_in, 16)
            for c in range(KD):
                act.wait_ge(*full(("xin", c)))
                src = bank(("xin", c))
                ins = act.copy(xT[:, c, :], src[:, 0:TOK])
                ins.then_inc(*was_read(("xin", c)))
            act.wait_ge(cols_ready, 1)
            act.activation(small[:, 0:16], pcol[:, 2 * N_PROW + 8:2 * N_PROW + 24], ACT.Exp, scale=-1.0)\
                .then_inc(setup_act, 1)
            act.wait_ge(tab_in, 16 * 8 * DEPTH)
            act.activation(a_exp, tab[:, :, T_AL:T_AL + DT], ACT.Exp).then_inc(setup_act, 1)

            for l in range(DEPTH):
                act.wait_ge(*taken(("h0", l)))

            def norm(l, n):
                if n:
                    for s in out_sem:
                        act.wait_ge(s, 16 * (l + 1))
                for j in range(4):
                    for c in (2 * j, 2 * j + 1):
                        act.wait_ge(*taken(("xin", c) if not (l or n) else ("wout", l, c) if n else ("sc", l - 1, PASSES - 1, c)))
                    ins = act.activation(sq[:, 2 * j:2 * j + 2, :], xT[:, 2 * j:2 * j + 2, :], ACT.Square)
                    ins.then_inc(sig["sq"], 1)
                key = ("ss", l, n)
                act.wait_ge(*full(key))
                src = bank(key)
                act.activation(lnrow, src[:, 0:TOK], ACT.Ln, bias=eps_col, scale=1.0 / D).then_inc(act_step, 1)
                act.wait_ge(act_step, act_steps())
                act.activation(src[:, 0:TOK], lnrow, ACT.Exp, scale=-0.5).then_inc(sig["rstd"], 1)

            act.wait_ge(setup_dve, 1)
            for l in range(DEPTH):
                for step in STEPS[l]:
                    kind, arg = step[0], step[1:]
                    if kind == "norm":
                        norm(l, arg[0])
                    elif kind == "xbc":
                        for c in range(6):
                            act.wait_ge(*taken(("xbc", l, c)))
                            act.activation(xbc[:, c, :], xbc[:, c, :], ACT.Silu).then_inc(sig["xbc_silu"], 1)
                        act.wait_ge(sig["dt_na"], per["dt_na"] * l + 1)
                        ins = act.activation(dtw[:, 1, :], dtw[:, 1, :], ACT.Exp)
                        ins.then_inc(sig["dt_u"], 1)
                        act.wait_ge(sig["dt_u"], per["dt_u"] * l + 1)
                        act.activation(dtw[:, 2, :], dtw[:, 1, :], ACT.Ln, bias=one_col).then_inc(sig["dt_r"], 1)
                    elif kind in ("rows", "rows_last"):
                        m = arg[0] if arg else TILES - 1
                        for g in range(3):
                            key = ("row", l, m, g)
                            act.wait_ge(*full(key))
                            src = bank(key)
                            if g == 2:
                                act.copy(z[:, m, :], src).then_inc(*was_read(key))
                                continue
                            act.copy(row[:, m, g * 512:g * 512 + 256].rearrange("p (b a d) -> p a b d", a=2, b=2),
                                     src[:, 0:256].rearrange("p (a b d) -> p a b d", a=2, b=2))
                            act.copy(row[:, m, g * 512 + 256:(g + 1) * 512], src[:, 256:512]).then_inc(*was_read(key))
                    elif kind == "prep":
                        m = arg[0]
                        act.wait_ge(sig["bss"], per["bss"] * l + m + 1)
                        act.activation(nrm[:, 8:14], nrm[:, 0:6], ACT.Ln, bias=eps_col, scale=1.0 / HD).then_inc(act_step, 1)
                        act.wait_ge(act_step, act_steps())
                        act.activation(nrm[:, 16:22], nrm[:, 8:14], ACT.Exp, scale=-0.5).then_inc(sig["brs"], 1)
                        if m == 0:
                            act.wait_ge(sig["prep"], per["prep"] * l + 1)
                            for i, c0 in enumerate((256, 384, OFF_B + 256, OFF_B + 384)):
                                act.dma_start(a_out[2 + i][0, l].rearrange("s k d -> s (k d)"), row[:, 0, c0:c0 + P])\
                                    .then_inc(out_sem[i], 16)
                    elif kind == "turn_qk":
                        m = arg[0]
                        for t in range(2):
                            key = ("qkT", l, m, t)
                            act.wait_ge(*full(key))
                            src = bank(key)[:, 0:3 * P].rearrange("p (c t) -> p c t", c=3)
                            act.copy(qkT[:, 3 * t:3 * t + 3, m * P:(m + 1) * P], src).then_inc(*was_read(key))
                    elif kind == "ssm_in":
                        m = arg[0]
                        key = ("xs", l, m)
                        act.wait_ge(*full(key))
                        src = bank(key)
                        if m:
                            act.wait_ge(sig["xd"], per["xd"] * l + m)
                        act.copy(xs, src).then_inc(*was_read(key))
                        key = ("cum", l, m)
                        act.wait_ge(*full(key))
                        src = bank(key)
                        ins = act.activation(ex[:, m, :], src[:, 0:48], ACT.Exp)
                        ins.then_inc(*was_read(key))
                    elif kind == "seg":
                        m = arg[0]
                        for d in range(2):
                            for g in range(2):
                                act.wait_ge(*full(("seg", l, m, d, g)))
                                src = bank(("seg", l, m, d, g))
                                act.activation(src, src, ACT.Exp).then_inc(sig["seg"], 1)
                    elif kind == "ssm_y":
                        if arg[0] == 0:
                            key = ("state", l, 0)
                            act.wait_ge(*full(key))
                            src = bank(key)
                            ins = act.copy(stout.rearrange("p a b n -> p (a b n)"), src)
                            ins.then_inc(*was_read(key))
                            act.wait_ge(*taken(key))
                            for d in range(2):
                                act.dma_start(a_out[6 + d][0, l].rearrange("(r h) p n -> (h p) r n", h=2),
                                              stout[:, d, :, :]).then_inc(out_sem[4 + d], 16)
                    elif kind == "silu_z":
                        for m in range(TILES):
                            act.wait_ge(*taken(("row", l, m, 2)))
                        act.activation(z, z, ACT.Silu).then_inc(sig["zs"], 1)
                    elif kind == "scores":
                        u = arg[0]
                        m, t, h = HEADS[u]
                        w = P if m == 0 else TOK
                        key = ("scores", l, u)
                        act.wait_ge(sig["nb"], per["nb"] * l + u + 1)
                        act.wait_ge(*full(key))
                        src = bank(key)
                        if u >= 4:
                            act.wait_ge(*full(("turn", l, u - 4)))
                        ins = act.activation(probs[:, u % 4, 0:w], src[:, 0:w], ACT.Exp, bias=att[:, 1, u:u + 1],
                                             scale=SCALE, accum_out=att[:, 2, u:u + 1])
                        ins.then_inc(*was_read(key))
                        if t == 0:
                            act.activation(att[:, 3, u:u + 1], nsink[:, l, h:h + 1], ACT.Exp,
                                                        bias=att[:, 1, u:u + 1], scale=-1.0).then_inc(sig["es"], 1)
                    elif kind == "turn" and HEADS[arg[0]][1] == 1:
                        turn_probs(act, act.copy, l, arg[0])
                    elif kind == "gate":
                        act.wait_ge(sig["yz"], per["yz"] * l + 1)
                        for m in range(TILES):
                            ins = act.activation(tmp[:, m, :], y[:, m, :], ACT.Square, accum_out=nrm[:, 24 + m:25 + m])
                        ins.then_inc(act_step, 1)
                        act.wait_ge(act_step, act_steps())
                        act.activation(nrm[:, 27:30], nrm[:, 24:27], ACT.Ln, bias=eps_col, scale=1.0 / DS).then_inc(act_step, 1)
                        act.wait_ge(act_step, act_steps())
                        act.activation(nrm[:, 27:30], nrm[:, 27:30], ACT.Exp, scale=-0.5).then_inc(sig["yrs"], 1)
                    elif kind == "turn_mix":
                        for c in range(4):
                            key = ("mix", l, c)
                            act.wait_ge(*full(key))
                            src = bank(key)
                            act.copy(hT[:, c, :], src[:, 0:TOK]).then_inc(*was_read(key))
                        for c in range(4, KD):
                            key = ("mix", l, c)
                            act.wait_ge(*full(key))
                            src = bank(key)
                            g = pcol[:, l * N_PROW + R_SG + c - 4:l * N_PROW + R_SG + c - 3]
                            act.activation(hT[:, c, :], src[:, 0:TOK], ACT.Copy, scale=g).then_inc(*was_read(key))
                    elif kind == "router":
                        act.wait_ge(sig["ge0"], per["ge0"] * l + 1)
                        act.activation(rt[:, 2, :, :], rt[:, 2, :, :], ACT.Exp).then_inc(sig["ge"], 1)
                        act.wait_ge(sig["ed0"], per["ed0"] * l + 1)
                        act.activation(rt[:, 3, :, 0:1], rt[:, 3, :, 0:1], ACT.Exp).then_inc(sig["ed"], 1)
                    elif kind == "hrow":
                        for m in range(TILES):
                            for half in range(2):
                                act.wait_ge(*full(("hrow", l, m, half)))
                                src = bank(("hrow", l, m, half)).rearrange("p (a t) -> p a t", t=8)
                                dst = h_hi[:, m, :, 64 * half:64 * half + 64].rearrange("p t a -> p a t")
                                act.copy(dst, src).then_inc(sig["hhi"], 1)
                    elif kind == "select":
                        p = arg[0]
                        if p:
                            act.wait_ge(*full(("sc", l, p - 1, KD - 1)))
                        for g in range(NG):
                            key = ("selT", l, p, g)
                            act.wait_ge(*full(key))
                            src = bank(key)
                            act.copy(selT[:, g, :], src[:, 0:TOK]).then_inc(*was_read(key))
                    elif kind == "gather":
                        p = arg[0]
                        for t in range(0, KD, 2):
                            gathered(act, act.copy, l, p, t)
                    elif kind == "gu":
                        p, e = arg
                        act.wait_ge(*full(("gu", l, p, e)))
                        src = bank(("gu", l, p, e))
                        if e >= 2:
                            act.wait_ge(*taken(("gu", l, p, e - 2)))
                        act.activation(sg[:, e % 2, :], src[:, 0:FE], ACT.Silu).then_inc(sig["sgl"], 1)
                    elif kind == "down":
                        p, e = arg
                        key = ("hidT", l, p, e)
                        act.wait_ge(*full(key))
                        src = bank(key)
                        act.copy(hidT[:, e % 2, :], src[:, 0:2 * P]).then_inc(*was_read(key))
                        if e % EPG == EPG - 1:
                            g = e // EPG
                            for half in range(2):
                                act.wait_ge(*full(("yg", l, p, g, half)))
                                src = bank(("yg", l, p, g, half))
                                act.copy(y_hi[:, g, half * 512:(half + 1) * 512], src).then_inc(sig["yhi"], 1)
            norm(DEPTH, 0)
            for m in range(TILES):
                for half in range(2):
                    key = ("out", m, half)
                    act.wait_ge(*full(key))
                    src = bank(key)
                    act.copy(row[:, m, half * 512:(half + 1) * 512], src).then_inc(*was_read(key))

        @block.vector
        def _(dve):

            tt, ts, stt = dve.tensor_tensor, dve.tensor_scalar, dve.scalar_tensor_tensor

            dve.memset(eps_col, EPS)
            dve.memset(one_col, 1.0).then_inc(dve_step, 1)
            dve.wait_ge(dve_step, dve_steps())
            dve.wait_ge(const_in, 16)
            dve.tensor_copy(ident_b, c_("ident"))
            dve.tensor_copy(mask_b, const[:, C_MASK:C_MASK + 2 * DEC].rearrange("p (b k) -> p b k", b=2))
            dve.wait_ge(tab_in, 16 * 8 * DEPTH)
            ts(nsink, tab[:, :, T_SINK:T_SINK + NH], -1.0, None, ALU.mult).then_inc(setup_dve, 1)
            key = ("pcol",)
            dve.wait_ge(*full(key))
            src = bank(key)
            dve.tensor_copy(pcol, src[:, 0:2 * N_PROW + 24]).then_inc(*was_read(key))
            dve.wait_ge(*taken(key))
            dve.sem_inc(cols_ready, 1)
            dve.wait_ge(setup_act, 1)
            ts(small[:, 0:16], small[:, 0:16], 1.0, None, ALU.add).then_inc(dve_step, 1)
            dve.wait_ge(dve_step, dve_steps())
            dve.reciprocal(small[:, 16:32], small[:, 0:16]).then_inc(dve_step, 1)
            dve.wait_ge(dve_step, dve_steps())
            tt(silu_c.rearrange("p k j -> p j k"), pcol[:, 2 * N_PROW + 8:2 * N_PROW + 24].rearrange("p (j k) -> p j k", j=2),
               small[:, 16:32].rearrange("p (j k) -> p j k", j=2), ALU.mult).then_inc(siluc_ready, 1)
            for l in range(DEPTH):
                key = ("ck", l)
                dve.wait_ge(*full(key))
                src = bank(key)
                dve.tensor_copy(ckT[:, l, :, :].rearrange("p t s -> p (t s)"), src[:, 0:2 * P]).then_inc(*was_read(key))
                key = ("h0", l)
                dve.wait_ge(*full(key))
                src = bank(key)
                dve.tensor_copy(h0T[:, l, :, :].rearrange("p t s -> p (t s)"), src).then_inc(*was_read(key))

            def ada(l, t):
                key = ("ada", l, t)
                dve.wait_ge(*full(key))
                src = bank(key)[:, 0:32].rearrange("p (c j) -> p c j", j=2)
                bias = pcol[:, l * N_PROW + R_BADA + 16 * t:l * N_PROW + R_BADA + 16 * (t + 1)]
                tt(mods[:, l, 16 * t:16 * (t + 1), :], src,
                                 bias.unsqueeze(2).to_broadcast((P, ADA_THIRD, 2)), ALU.add).then_inc(*was_read(key))
                dve.wait_ge(*taken(key))
                if t != 1:
                    n = t // 2
                    sc = (SC1, SC2)[n]
                    gain = pcol[:, l * N_PROW + (R_N1, R_N2)[n]:l * N_PROW + (R_N1, R_N2)[n] + KD]
                    stt(amul[:, l, n, :, :], mods[:, l, sc:sc + KD, :], 1.0,
                             gain.unsqueeze(2).to_broadcast((P, KD, 2)), ALU.add, ALU.mult).then_inc(dve_step, 1)
                    dve.wait_ge(dve_step, dve_steps())

            ada(0, 0)

            def norm(l, n):
                key = ("ss", l, n)
                dve.wait_ge(sig["rstd"], 2 * l + n + 1)
                dve.wait_ge(*full(key))
                src = bank(key)[:, 0:TOK].unsqueeze(1).to_broadcast((P, 4, TOK))
                for half in range(2):
                    ins = tt(hT[:, 4 * half:4 * half + 4, :], xT[:, 4 * half:4 * half + 4, :], src, ALU.mult)
                    if half:
                        ins.then_inc(*was_read(key))
                        dve.wait_ge(*taken(key))
                    else:
                        ins.then_inc(dve_step, 1)
                        dve.wait_ge(dve_step, dve_steps())
                    for c in range(4 * half, 4 * half + 4):
                        if l == DEPTH:
                            ts(hT[:, c, :], hT[:, c, :], pcol[:, 2 * N_PROW + c:2 * N_PROW + c + 1],
                                           None, ALU.mult).then_inc(sig["h"], 1)
                            continue
                        for j, part in ((0, slice(0, P)), (1, slice(P, TOK))):
                            ins = ts(hT[:, c, part], hT[:, c, part], amul[:, l, n, c, j:j + 1],
                                     mods[:, l, (SH1, SH2)[n] + c, j:j + 1], ALU.mult, ALU.add)
                        ins.then_inc(sig["h"], 1)

            def residual(key, c, l, gate):
                dve.wait_ge(*full(key))
                src = bank(key)
                for j, part in ((0, slice(0, P)), (1, slice(P, TOK))):
                    ins = stt(xT[:, c, part], src[:, part], mods[:, l, gate + c, j:j + 1], xT[:, c, part],
                              ALU.mult, ALU.add)
                ins.then_inc(*was_read(key))

            def rope(m, at):
                x = row[:, m, at:at + 6 * HD]
                cos = const[:, C_COS + HD * (m - 1):C_COS + HD * m]
                sin = const[:, C_SIN + HD * (m - 1):C_SIN + HD * m].rearrange("p (f q d) -> p f q d", f=2, q=2)
                xh = x.rearrange("p (h d) -> p h d", d=HD)
                t1, t2 = tmp[:, 0, 0:6 * HD], tmp[:, 1, 0:6 * HD]
                tt(t1.rearrange("p (h d) -> p h d", d=HD), xh, cos.unsqueeze(1).to_broadcast((P, 6, HD)), ALU.mult)
                xq = x.rearrange("p (h f q d) -> p h f q d", h=6, f=2, q=2)
                tq = t2.rearrange("p (h f q d) -> p h f q d", h=6, f=2, q=2)
                for q in range(2):
                    ins = tt(tq[:, :, :, q, :], xq[:, :, :, 1 - q, :],
                             sin[:, :, q, :].unsqueeze(1).to_broadcast((P, 6, 2, 16)), ALU.mult)
                ins.then_inc(dve_step, 1)
                dve.wait_ge(dve_step, dve_steps())
                return tt(x, t1, t2, ALU.add)

            def first_of(out, eq, scratch, mi):
                iota4 = c_("iota", 4).unsqueeze(1).to_broadcast((P, TILES, 4))
                stt(scratch, eq, -100.0, iota4, ALU.mult, ALU.add).then_inc(dve_step, 1)
                dve.wait_ge(dve_step, dve_steps())
                dve.tensor_reduce(mi, scratch, AX.X, ALU.min).then_inc(dve_step, 1)
                dve.wait_ge(dve_step, dve_steps())
                return tt(out, scratch, mi.to_broadcast((P, TILES, 4)), ALU.is_equal)

            for l in range(DEPTH):
                for step in STEPS[l]:
                    kind, arg = step[0], step[1:]
                    if kind == "norm":
                        norm(l, arg[0])
                    elif kind == "ada":
                        if arg[2] == KD - 1:
                            ada(arg[0], arg[1])
                    elif kind == "xbc":
                        key = ("dt", l)
                        dve.wait_ge(*full(key))
                        src = bank(key)
                        bias = tab[:, l, T_DTB:T_DTB + DT].unsqueeze(1).to_broadcast((P, TILES, DT))
                        tt(dtw[:, 0, :].rearrange("p (m n) -> p m n", n=DT),
                                         src[:, 0:TILES * DT].rearrange("p (m n) -> p m n", n=DT), bias, ALU.add).then_inc(*was_read(key))
                        dve.wait_ge(*taken(key))
                        stt(dtw[:, 1, :], dtw[:, 0, :], -1.0, dtw[:, 0, :], ALU.mult, ALU.min).then_inc(sig["dt_na"], 1)
                        for c in range(6):
                            key = ("xbc", l, c)
                            dve.wait_ge(*full(key))
                            src = bank(key)
                            cw = [pcol[:, l * N_PROW + R_CW + 6 * t + c:l * N_PROW + R_CW + 6 * t + c + 1] for t in range(3)]
                            cb = pcol[:, l * N_PROW + R_CB + c:l * N_PROW + R_CB + c + 1]
                            ts(xbc[:, c, :], src[:, 0:TOK], cw[1], cb, ALU.mult, ALU.add).then_inc(dve_step, 1)
                            dve.wait_ge(dve_step, dve_steps())
                            for b0, b1 in ((0, P), (P, TOK)):
                                ins = stt(xbc[:, c, b0 + 1:b1], src[:, b0:b1 - 1], cw[0], xbc[:, c, b0 + 1:b1],
                                          ALU.mult, ALU.add)
                            ins.then_inc(dve_step, 1)
                            dve.wait_ge(dve_step, dve_steps())
                            stt(xbc[:, c, 0:P - 1], src[:, 1:P], cw[2], xbc[:, c, 0:P - 1], ALU.mult, ALU.add)
                            stt(xbc[:, c, P:TOK - 1], src[:, P + 1:TOK], cw[2], xbc[:, c, P:TOK - 1],
                                              ALU.mult, ALU.add).then_inc(*was_read(key))
                        dve.wait_ge(sig["dt_u"], per["dt_u"] * l + 1)
                        ts(dtw[:, 3, :], dtw[:, 1, :], 1.0, -1.0, ALU.add, ALU.add)
                        ts(dtw[:, 4, :], dtw[:, 1, :], 1.0, None, ALU.add).then_inc(dve_step, 1)
                        dve.wait_ge(dve_step, dve_steps())
                        tt(dtw[:, 3, :], dtw[:, 1, :], dtw[:, 3, :], ALU.subtract)
                        dve.reciprocal(dtw[:, 5, :], dtw[:, 4, :]).then_inc(dve_step, 1)
                        dve.wait_ge(dve_step, dve_steps())
                        tt(dtw[:, 3, :], dtw[:, 3, :], dtw[:, 5, :], ALU.mult).then_inc(dve_step, 1)
                        dve.wait_ge(dve_step, dve_steps())
                        dve.wait_ge(sig["dt_r"], per["dt_r"] * l + 1)
                        tt(dtw[:, 3, :], dtw[:, 3, :], dtw[:, 2, :], ALU.add).then_inc(dve_step, 1)
                        dve.wait_ge(dve_step, dve_steps())
                        stt(dts.rearrange("p m n -> p (m n)"), dtw[:, 0, :], 0.0, dtw[:, 3, :], ALU.max, ALU.add).then_inc(dve_step, 1)
                        dve.wait_ge(dve_step, dve_steps())
                        if l == 0:
                            dve.wait_ge(setup_act, 2)
                        stt(dav, dts, -1.0, a_exp[:, l, :].unsqueeze(1).to_broadcast((P, TILES, DT)),
                                         ALU.mult, ALU.mult).then_inc(sig["da"], 1)
                    elif kind == "prep":
                        m = arg[0]
                        dve.wait_ge(*taken(("row", l, m, 0)))
                        dve.wait_ge(*taken(("row", l, m, 1)))
                        b6 = row[:, m, OFF_B:OFF_B + 6 * HD]
                        b6h = b6.rearrange("p (h d) -> p h d", d=HD)
                        tt(tmp[:, 2, 0:6 * HD], b6, b6, ALU.mult).then_inc(dve_step, 1)
                        dve.wait_ge(dve_step, dve_steps())
                        dve.tensor_reduce(nrm[:, 0:6], tmp[:, 2, 0:6 * HD].rearrange("p (h d) -> p h d", d=HD),
                                                        AX.X, ALU.add).then_inc(sig["bss"], 1)
                        if m:
                            rope(m, 0).then_inc(dve_step, 1)
                            dve.wait_ge(dve_step, dve_steps())
                        dve.wait_ge(sig["brs"], per["brs"] * l + m + 1)
                        tt(b6h, b6h, nrm[:, 16:22].unsqueeze(2).to_broadcast((P, 6, HD)), ALU.mult).then_inc(dve_step, 1)
                        dve.wait_ge(dve_step, dve_steps())
                        ins = tt(b6, b6, tab[:, l, T_GQK:T_GQK + 6 * HD], ALU.mult)
                        if m:
                            ins.then_inc(dve_step, 1)
                            dve.wait_ge(dve_step, dve_steps())
                            ins = rope(m, OFF_B)
                        ins.then_inc(sig["prep"], 1)
                    elif kind == "ssm_in":
                        m = arg[0]
                        key = ("bg", l, m)
                        dve.wait_ge(*full(key))
                        src = bank(key)
                        if m:
                            dve.wait_ge(*full(("state", l, m - 1)))
                        dve.tensor_copy(bro, src[:, 0:P])
                        for g in range(2):
                            if g:
                                key = ("bg1", l, m)
                                dve.wait_ge(*full(key))
                                src = bank(key)
                            tt(gm[:, 0, g, :], src[:, P:2 * P], c_("incl_f"), ALU.mult)
                            tt(gm[:, 1, g, :], src[:, P:2 * P], c_("incl_b"), ALU.mult).then_inc(*was_read(key))
                    elif kind == "seg":
                        m = arg[0]
                        dve.wait_ge(*taken(("bg", l, m)))
                        dve.wait_ge(*taken(("bg1", l, m)))
                        for d in range(2):
                            for g in range(2):
                                key = ("seg", l, m, d, g)
                                dve.wait_ge(sig["seg"], per["seg"] * l + 4 * m + 2 * d + g + 1)
                                src = psum[:, uses[key][0], :].rearrange("p (h t) -> p h t", h=4)
                                tt(mm[:, d, 4 * g:4 * g + 4, :], src,
                                                 gm[:, d, g, :].unsqueeze(1).to_broadcast((P, 4, P)), ALU.mult).then_inc(*was_read(key))
                    elif kind == "ssm_y":
                        m = arg[0]
                        key = ("ydiag", l, m)
                        dve.wait_ge(sig["yx"], per["yx"] * l + m + 1)
                        dve.wait_ge(*full(key))
                        src = bank(key)
                        tt(y[:, m, :], src, yx, ALU.add).then_inc(*was_read(key))
                        if m:
                            d = m - 1
                            key = ("state", l, m)
                            dve.wait_ge(*taken(("cum", l, m)))
                            dve.wait_ge(*taken(("h0", l)))
                            for g in range(2):
                                part = slice(64 * g, 64 * g + 64)
                                total = ex[part, m, 32 + 8 * d + 4 * g:32 + 8 * d + 4 * g + 4]
                                ins = tt(hin[part, d, :].rearrange("p (h n) -> p h n", h=4),
                                         h0T[part, l, d, :].rearrange("p (h n) -> p h n", h=4),
                                         total.unsqueeze(2).to_broadcast((64, 4, HD)), ALU.mult)
                            ins.then_inc(dve_step, 1)
                            dve.wait_ge(dve_step, dve_steps())
                            dve.wait_ge(*full(key))
                            src = bank(key)
                            tt(hin[:, d, :], src[:, 0:256], hin[:, d, :], ALU.add).then_inc(*was_read(key))
                    elif kind == "ssm_off":
                        m = arg[0]
                        dve.wait_ge(*taken(("ydiag", l, m)))
                        for g in range(2):
                            key = ("yoff", l, m, g)
                            dve.wait_ge(*full(key))
                            src = bank(key).rearrange("p (d h n) -> p d h n", d=2, h=4)
                            dec = ex[:, m, 0:16].rearrange("p (d h) -> p d h", d=2)[:, :, 4 * g:4 * g + 4]
                            tt(tmp[:, g, :].rearrange("p (d h n) -> p d h n", d=2, h=4), src,
                                             dec.unsqueeze(3).to_broadcast((P, 2, 4, HD)), ALU.mult).then_inc(*was_read(key))
                        dve.wait_ge(*taken(("yoff", l, m, 0)))
                        dve.wait_ge(*taken(("yoff", l, m, 1)))
                        ym = y[:, m, :].rearrange("p (g n) -> p g n", g=2)
                        for d in range(2):
                            tt(ym, ym, tmp[:, 0:2, d * 256:(d + 1) * 256], ALU.add).then_inc(dve_step, 1)
                            dve.wait_ge(dve_step, dve_steps())
                    elif kind == "scores":
                        u = arg[0]
                        m, t, h = HEADS[u]
                        dve.wait_ge(*full(("scores", l, u)))
                        src = bank(("scores", l, u))
                        dve.tensor_reduce(att[:, 0, u:u + 1], src[:, 0:P if m == 0 else TOK], AX.X, ALU.max,
                                               negate=True).then_inc(dve_step, 1)
                        dve.wait_ge(dve_step, dve_steps())
                        if t == 0:
                            ins = ts(att[:, 1, u:u + 1], att[:, 0, u:u + 1], SCALE, nsink[:, l, h:h + 1],
                                     ALU.mult, ALU.min)
                        else:
                            ins = ts(att[:, 1, u:u + 1], att[:, 0, u:u + 1], SCALE, None, ALU.mult)
                        ins.then_inc(sig["nb"], 1)
                    elif kind == "turn" and HEADS[arg[0]][1] == 0:
                        turn_probs(dve, dve.tensor_copy, l, arg[0])
                    elif kind == "values":
                        u = arg[0]
                        m, t, h = HEADS[u]
                        den = att[:, 2, u:u + 1]
                        if t == 0:
                            dve.wait_ge(sig["es"], per["es"] * l + sum(1 for x in HEADS[:u + 1] if x[1] == 0))
                            tt(att[:, 4, u:u + 1], den, att[:, 3, u:u + 1], ALU.add).then_inc(dve_step, 1)
                            dve.wait_ge(dve_step, dve_steps())
                            den = att[:, 4, u:u + 1]
                        else:
                            dve.wait_ge(*taken(("scores", l, u)))
                        dve.reciprocal(att[:, 5, u:u + 1], den).then_inc(dve_step, 1)
                        dve.wait_ge(dve_step, dve_steps())
                        key = ("values", l, u)
                        dve.wait_ge(*full(key))
                        src = bank(key)
                        ts(row[:, m, t * OFF_B + h * HD:t * OFF_B + (h + 1) * HD], src[:, 0:HD],
                                         att[:, 5, u:u + 1], None, ALU.mult).then_inc(*was_read(key))
                    elif kind == "gate":
                        dve.wait_ge(sig["zs"], per["zs"] * l + 1)
                        dve.wait_ge(*taken(("ydiag", l, 0)))
                        tt(y, y, z, ALU.mult).then_inc(sig["yz"], 1)
                        dve.wait_ge(sig["yrs"], per["yrs"] * l + 1)
                        for m in range(TILES):
                            ins = ts(y[:, m, :], y[:, m, :], nrm[:, 27 + m:28 + m], None, ALU.mult)
                        ins.then_inc(sig["yn"], 1)
                    elif kind == "wout":
                        for c in range(KD):
                            residual(("wout", l, c), c, l, G1)
                    elif kind == "router":
                        key = ("logits", l)
                        dve.wait_ge(*full(key))
                        src = bank(key)
                        n = NG + NE
                        bias = tab[:, l, T_BG:T_BG + n].unsqueeze(1).to_broadcast((P, TILES, n))
                        tt(lg, src[:, 0:TILES * n].rearrange("p (m n) -> p m n", n=n), bias, ALU.add).then_inc(*was_read(key))
                        dve.wait_ge(*taken(key))
                        col = lambda i, j: rt[:, i, :, j:j + 1]
                        bc = lambda v: v.to_broadcast((P, TILES, 4))
                        dve.tensor_reduce(col(6, 0), lg[:, :, 0:NG], AX.X, ALU.max).then_inc(dve_step, 1)
                        dve.wait_ge(dve_step, dve_steps())
                        tt(rt[:, 2, :, :], lg[:, :, 0:NG], bc(col(6, 0)), ALU.subtract).then_inc(sig["ge0"], 1)
                        tt(rt[:, 8, :, :], lg[:, :, 0:NG], bc(col(6, 0)), ALU.is_equal).then_inc(dve_step, 1)
                        dve.wait_ge(dve_step, dve_steps())
                        first_of(rt[:, 0, :, :], rt[:, 8, :, :], rt[:, 9, :, :], col(6, 1)).then_inc(sig["goh"], 1)
                        dve.wait_ge(sig["goh"], per["goh"] * l + 1)
                        tt(e16.rearrange("p m (g j) -> p m g j", g=NG),
                                lg[:, :, NG:n].rearrange("p m (g j) -> p m g j", g=NG),
                                rt[:, 0, :, :].unsqueeze(3).to_broadcast((P, TILES, NG, EPG)), ALU.mult).then_inc(dve_step, 1)
                        dve.wait_ge(dve_step, dve_steps())
                        dve.tensor_reduce(rt[:, 10, :, :], e16.rearrange("p m (g j) -> p m j g", g=NG), AX.X, ALU.add).then_inc(dve_step, 1)
                        dve.wait_ge(dve_step, dve_steps())
                        dve.tensor_reduce(col(6, 2), rt[:, 10, :, :], AX.X, ALU.max).then_inc(dve_step, 1)
                        dve.wait_ge(dve_step, dve_steps())
                        tt(rt[:, 8, :, :], rt[:, 10, :, :], bc(col(6, 2)), ALU.is_equal).then_inc(dve_step, 1)
                        dve.wait_ge(dve_step, dve_steps())
                        first_of(rt[:, 11, :, :], rt[:, 8, :, :], rt[:, 9, :, :], col(6, 3)).then_inc(dve_step, 1)
                        dve.wait_ge(dve_step, dve_steps())
                        stt(rt[:, 12, :, :], rt[:, 11, :, :], -BIG, rt[:, 10, :, :], ALU.mult, ALU.add).then_inc(dve_step, 1)
                        dve.wait_ge(dve_step, dve_steps())
                        dve.tensor_reduce(col(13, 0), rt[:, 12, :, :], AX.X, ALU.max).then_inc(dve_step, 1)
                        dve.wait_ge(dve_step, dve_steps())
                        tt(col(3, 0), col(13, 0), col(6, 2), ALU.subtract).then_inc(sig["ed0"], 1)
                        tt(rt[:, 8, :, :], rt[:, 12, :, :], bc(col(13, 0)), ALU.is_equal).then_inc(dve_step, 1)
                        dve.wait_ge(dve_step, dve_steps())
                        first_of(rt[:, 14, :, :], rt[:, 8, :, :], rt[:, 9, :, :], col(13, 1)).then_inc(dve_step, 1)
                        dve.wait_ge(dve_step, dve_steps())
                        dve.wait_ge(sig["ge"], per["ge"] * l + 1)
                        dve.tensor_reduce(col(13, 2), rt[:, 2, :, :], AX.X, ALU.add).then_inc(dve_step, 1)
                        dve.wait_ge(dve_step, dve_steps())
                        dve.wait_ge(sig["ed"], per["ed"] * l + 1)
                        stt(col(15, 0), col(3, 0), 1.0, col(13, 2), ALU.add, ALU.mult).then_inc(dve_step, 1)
                        dve.wait_ge(dve_step, dve_steps())
                        dve.reciprocal(col(15, 1), col(15, 0)).then_inc(dve_step, 1)
                        dve.wait_ge(dve_step, dve_steps())
                        tt(col(15, 2), col(15, 1), col(3, 0), ALU.mult).then_inc(dve_step, 1)
                        dve.wait_ge(dve_step, dve_steps())
                        tt(rt[:, 16, :, :], rt[:, 11, :, :], bc(col(15, 1)), ALU.mult)
                        tt(rt[:, 17, :, :], rt[:, 14, :, :], bc(col(15, 2)), ALU.mult).then_inc(dve_step, 1)
                        dve.wait_ge(dve_step, dve_steps())
                        tt(rt[:, 1, :, :], rt[:, 16, :, :], rt[:, 17, :, :], ALU.add).then_inc(sig["cw"], 1)
                    elif kind == "hrow":
                        for m in range(TILES):
                            for half in range(2):
                                key = ("hrow", l, m, half)
                                dve.wait_ge(sig["hhi"], per["hhi"] * l + 2 * m + half + 1)
                                dve.wait_ge(*full(key))
                                src = bank(key).rearrange("p (a t) -> p a t", t=8)
                                part = slice(64 * half, 64 * half + 64)
                                tt(h_lo[:, m, :, part].rearrange("p t a -> p a t"), src,
                                                 h_hi[:, m, :, part].bitcast(F32).rearrange("p t a -> p a t"),
                                                 ALU.subtract).then_inc(*was_read(key))
                    elif kind == "rank":
                        key = ("rank", l)
                        dve.wait_ge(*full(key))
                        src = bank(key)[:, 0:TILES * NG].rearrange("p (m g) -> p m g", g=NG)
                        stt(rt[:, 4, :, :], src, 1.0, rt[:, 0, :, :], ALU.add, ALU.mult).then_inc(*was_read(key))
                        dve.wait_ge(*taken(key))
                    elif kind == "select":
                        p = arg[0]
                        ts(rt[:, 5, :, :], rt[:, 4, :, :], -1.0 - P * p, None, ALU.add).then_inc(dve_step, 1)
                        dve.wait_ge(dve_step, dve_steps())
                        if p:
                            dve.wait_ge(*full(("xg", l, p - 1, KD - 1)))
                        for m in range(TILES):
                            for g in range(NG):
                                ins = ts(sel[:, m, g, :], c_("iota"), rt[:, 5, m, g:g + 1], None, ALU.is_equal)
                        ins.then_inc(sig["sel"], 1)
                        key = ("cwg", l, p)
                        dve.wait_ge(*full(key))
                        src = bank(key)
                        dve.tensor_copy(cwg.rearrange("p g j -> p (g j)"), src[:, 0:NE]).then_inc(*was_read(key))
                        dve.wait_ge(*taken(key))
                    elif kind == "gather":
                        p = arg[0]
                        for t in range(1, KD, 2):
                            gathered(dve, dve.tensor_copy, l, p, t)
                    elif kind == "gu":
                        p, e = arg
                        key = ("gu", l, p, e)
                        dve.wait_ge(sig["sgl"], per["sgl"] * l + NE * p + e + 1)
                        if e >= 2:
                            dve.wait_ge(*full(("hidT", l, p, e - 2)))
                        src = psum[:, uses[key][0], :]
                        stt(hid[:, e % 2, :], sg[:, e % 2, :], cwg[:, e // EPG, e % EPG:e % EPG + 1],
                                          src[:, FE:2 * FE], ALU.mult, ALU.mult).then_inc(*was_read(key))
                    elif kind == "down":
                        p, e = arg
                        if e % EPG == EPG - 1:
                            g = e // EPG
                            for half in range(2):
                                key = ("yg", l, p, g, half)
                                part = slice(half * 512, (half + 1) * 512)
                                dve.wait_ge(sig["yhi"], per["yhi"] * l + 8 * p + 2 * g + half + 1)
                                tt(y_lo[:, g, part], psum[:, uses[key][0], :],
                                                 y_hi[:, g, part].bitcast(F32), ALU.subtract).then_inc(*was_read(key))
                    elif kind == "scatter":
                        for c in range(KD):
                            residual(("sc", l, arg[0], c), c, l, G2)
            norm(DEPTH, 0)

        @block.gpsimd
        def _(pool):

            tt = pool.tensor_tensor
            pool.wait_ge(const_in, 16)
            pool.wait_ge(tab_in, 16 * 8 * DEPTH)
            for l in range(DEPTH):
                for step in STEPS[l]:
                    if step[0] != "ssm_in":
                        continue
                    m = step[1]
                    pool.wait_ge(sig["da"], per["da"] * l + 1)
                    if m:
                        pool.wait_ge(*full(("seg", l, m - 1, 1, 1)))
                    for d, tri in enumerate(("incl_f", "incl_b")):
                        ins = tt(ud[:, d, :, :], c_(tri).unsqueeze(1).to_broadcast((P, SH, P)),
                                 dav[:, m, 8 * d:8 * d + 8].unsqueeze(2).to_broadcast((P, SH, P)), ALU.mult)
                    ins.then_inc(sig["ud"], 1)
                    pool.wait_ge(*taken(("xs", l, m)))
                    pool.wait_ge(*taken(("cum", l, m)))
                    if m:
                        pool.wait_ge(*taken(("ydiag", l, m - 1)))
                    xh = xs.rearrange("p (h n) -> p h n", h=SH)
                    tt(yx.rearrange("p (h n) -> p h n", h=SH), xh,
                                    tab[:, l, T_DSK:T_DSK + SH].unsqueeze(2).to_broadcast((P, SH, HD)), ALU.mult).then_inc(sig["yx"], 1)
                    if m:
                        pool.wait_ge(*full(("state", l, m - 1)))
                    for d in range(2):
                        ins = tt(xd[:, d, :, :], xh,
                                 dts[:, m, 8 * d:8 * d + 8].unsqueeze(2).to_broadcast((P, SH, HD)), ALU.mult)
                    ins.then_inc(pool_step, 1)
                    pool.wait_ge(pool_step, pool_steps())
                    for d in range(2):
                        ins = tt(xdd[:, d, :, :], xd[:, d, :, :],
                                 ex[:, m, 16 + 8 * d:24 + 8 * d].unsqueeze(2).to_broadcast((P, SH, HD)), ALU.mult)
                    ins.then_inc(sig["xd"], 1)


_INS = ["x_prompt", "x_sample", "cache_a_k", "cache_a_v", "cache_b_k", "cache_b_v", "state_ssm_fwd",
        "state_ssm_bwd", "c", "c_ctx", "norm1_g", "norm2_g", "final_norm_g", "w_ada", "b_ada", "w_in", "a_sink",
        "q_norm_g", "k_norm_g", "conv_w", "conv_b", "dt_bias", "a_log", "d_skip", "ssm_norm_g", "w_out",
        "w_router_group", "b_router_group", "w_router_expert", "b_router_expert", "w_gate", "w_up", "w_down"]
_OUTS = [(1, SEQ, D), (1, DEC, D)] + [(1, DEPTH, SEQ, NKV, HD)] * 4 + [(1, DEPTH, SH, HD, 64)] * 2


def kernel(**inputs):
    import concourse.bacc as bacc
    from concourse.bass_utils import run_bass_kernel_spmd as run

    nc = bacc.Bacc("TRN2", target_bir_lowering=False, num_devices=1)
    arrays = {n: np.ascontiguousarray(inputs[n]) for n in _INS}
    arrays["const"] = constants()
    a = {n: nc.dram_tensor("in_" + n, v.shape, F32, kind="ExternalInput").ap() for n, v in arrays.items()}
    outs = [nc.dram_tensor(f"out_{i}", s, F32, kind="ExternalOutput").ap() for i, s in enumerate(_OUTS)]
    build(nc, a, outs)
    r = run(nc, [{"in_" + n: v for n, v in arrays.items()}], core_ids=[0])
    return tuple(r.results[0][f"out_{i}"] for i in range(len(_OUTS)))
```

```python
from contextlib import ExitStack

import numpy as np

import concourse.bass as bass
from concourse import mybir
from concourse.alu_op_type import AluOpType as ALU

ACT = mybir.ActivationFunctionType
F32 = mybir.dt.float32
F32R = mybir.dt.float32r
BF16 = mybir.dt.bfloat16
I32 = mybir.dt.int32
AX = mybir.AxisListType

P = 128
DEPTH, D, SEQ, DEC = 2, 1024, 128, 256
KD = D // P
TILES = (SEQ + DEC) // P
TOK = TILES * P
HD = 64
NH, NKV = 4, 2
SH, SG, DS = 8, 2, 512
XBC, DT = 768, 16
D_IN = 2320
OFF_B, OFF_Z, OFF_XBC, OFF_DT = 512, 1024, 1536, 2304
NG, EPG, FE = 4, 4, 256
NE = NG * EPG
EPS = 1e-6
SCALE = HD ** -0.5
BIG = 1e30
PIECE = 2048
RING = 8
WINDOW = 128
SH1, SC1, G1, SH2, SC2, G2 = (8 * i for i in range(6))

R_N1, R_N2, R_BADA, R_CW, R_CB, R_SG = 0, 8, 16, 64, 82, 88
N_PROW = 92
T_DTB, T_AL, T_DSK, T_SINK, T_BG, T_BE, T_GQK = 0, 16, 32, 40, 44, 48, 64
N_TAB = T_GQK + 6 * HD
names = ["ident", "incl_f", "incl_b", "after", "before", "ones", "iota"]
C_AT = {n: P * i for i, n in enumerate(names)}
C_MASK = P * len(names)
C_COS = C_MASK + 2 * DEC
C_SIN = C_COS + 2 * HD
N_CONST = C_SIN + 2 * HD


def constants():
    k, c = np.arange(P)[:, None], np.arange(P)[None, :]
    t = np.zeros((P, N_CONST), np.float32)
    for n, v in (("ident", k == c), ("incl_f", k <= c), ("incl_b", k >= c), ("after", k > c),
                 ("before", k < c), ("ones", k == k + 0 * c), ("iota", c + 0 * k)):
        t[:, C_AT[n]:C_AT[n] + P] = v
    key = np.arange(DEC)[None, :]
    for b in range(2):
        t[:, C_MASK + DEC * b:C_MASK + DEC * (b + 1)] = np.where(np.abs(key - (b * P + k)) <= WINDOW, 0.0, -BIG)
    quarter = HD // 4
    inv = (10000.0 ** (-np.arange(quarter, dtype=np.float32) / quarter)).astype(np.float32)
    for b in range(2):
        pos = b * P + np.arange(P)
        r, w = (pos // 64).astype(np.float32)[:, None] * inv, (pos % 64).astype(np.float32)[:, None] * inv
        ang = np.concatenate([r, r, w, w], 1)
        sign = np.repeat(np.array([-1, 1, -1, 1], np.float32), quarter)
        t[:, C_COS + HD * b:C_COS + HD * (b + 1)] = np.cos(ang)
        t[:, C_SIN + HD * b:C_SIN + HD * (b + 1)] = np.sin(ang) * sign
    return t


HEADS = [(m, t, h) for m in (1, 2, 0) for t in range(2) for h in range(NH)]


def head_steps():
    n = len(HEADS)
    out = []
    for u in range(n + 3):
        if u < n:
            out.append(("scores", u))
        if 2 <= u < n + 2:
            out.append(("turn", u - 2))
        if u >= 3:
            out.append(("values", u - 3))
    return out


def moe_steps(p):
    s = [("select", p), ("gather", p)]
    for e in range(NE):
        s.append(("gate_half", p, e))
        if e:
            s += [("split", p, e - 1), ("turn_hid", p, e - 1)]
        s.append(("gu", p, e))
        if e:
            s.append(("down", p, e - 1))
    return s + [("split", p, NE - 1), ("turn_hid", p, NE - 1), ("down", p, NE - 1), ("scatter", p)]


def more_steps():
    return [s for p in range(1, TILES) for s in moe_steps(p)]


def layer_steps(l):
    ada = [("ada", l, t, k) for t in (1, 2) for k in range(KD)]
    ahead = [("ada", l + 1, 0, k) for k in range(KD)] if l + 1 < DEPTH else []
    s = [("norm", 0)] + ada[:3] + [("xbc",)] + ([("caches",)] if l == 0 else [])
    s += [("rows", 0), ("ssm_in", 0), ("prep", 0), ("seg", 0), ("rows", 1), ("ssm_y", 0),
         ("ssm_in", 1), ("turn_qk", 0), ("seg", 1), ("prep", 1), ("rows_last",), ("ssm_y", 1), ("ssm_in", 2),
         ("turn_qk", 1), ("prep", 2), ("seg", 2), ("silu_z",)]
    s += [("ssm_y", 2), ("turn_qk", 2), ("ssm_off", 1), ("ssm_off", 2)]
    heads = head_steps()
    rest = ada[3:8] + [("ada_turn", l, 1)] + ada[8:14]
    done = 0
    for i, h in enumerate(heads):
        s.append(h)
        want = len(rest) * (i + 1) // len(heads)
        s += rest[done:want]
        done = want
    s += [("gate",)] + ada[14:] + [("turn_mix",), ("ada_turn", l, 2), ("wout",), ("norm", 1)] + ahead[:3]
    s += [("router",), ("hrow",)] + ahead[3:6] + [("rank",)] + ahead[6:]
    if ahead:
        s.append(("ada_turn", l + 1, 0))
    return s + moe_steps(0) + [("more",)]


def build(nc, a, a_out):
    PASSES = TILES
    pieces = [("ada", 0, 0, k) for k in range(KD)]
    more_pieces = []
    STEPS = [layer_steps(l) for l in range(DEPTH)]
    for l in range(DEPTH):
        for s in STEPS[l]:
            if s[0] == "xbc":
                pieces += [("xbc", l, i) for i in range(KD // 2)] + [("win", l, k) for k in range(KD)]
            elif s[0] == "ada":
                pieces.append(s)
            elif s[0] == "wout":
                pieces += [("wout", l, i) for i in range(KD // 2)]
            elif s[0] == "gate_half":
                pieces.append(("gate", l, *s[1:]))
            elif s[0] == "gu":
                pieces.append(("up", l, *s[1:]))
            elif s[0] == "down":
                pieces.append(("down", l, *s[1:]))
    for s in more_steps():
        if s[0] == "gate_half":
            more_pieces.append(("gate", *s[1:]))
        elif s[0] == "gu":
            more_pieces.append(("up", *s[1:]))
        elif s[0] == "down":
            more_pieces.append(s)
    piece_at = {key: n for n, key in enumerate(pieces)}
    for l in range(DEPTH):
        piece_at.update({(key[0], l, *key[1:]): n for n, key in enumerate(more_pieces)})

    with ExitStack() as ctx:
        def sb(name, shape, dt=F32, c=ctx):
            return c.enter_context(nc.sbuf_tensor(name, shape, dt))[:]

        all_sems = {}

        def sem(name):
            all_sems[name] = ctx.enter_context(nc.semaphore(name))
            return all_sems[name]

        def counter():
            n = [0]

            def more():
                n[0] += 1
                return n[0]
            return more

        xT = sb("xT", [P, KD, TOK])
        with ExitStack() as shared:
            hT = sb("hT", [P, KD, TOK], c=shared)
        down_hi = sb("down_hi", [P, PIECE], F32R)
        hidT_lo = sb("hidT_lo", [P, 2, FE], F32R)
        sb("hT_rest", [P, KD * TOK - PIECE - 2 * FE])
        ring = sb("ring", [P, RING, PIECE])
        const = sb("const", [P, N_CONST])
        pcol = sb("pcol", [P, 2 * N_PROW + 24])
        tab = sb("tab", [P, DEPTH, N_TAB])
        silu_c = sb("silu_c", [P, KD, 32])
        ada_rows = sb("ada_rows", [P, 512])
        prow = ada_rows[:, 0:3 * P].rearrange("p (i c) -> p i c", i=3)
        mods = sb("mods", [P, DEPTH, 48, 2])
        amul = sb("amul", [P, DEPTH, 2, KD, 2])
        eps_col = sb("eps_col", [P, 1])
        one_col = sb("one_col", [P, 1])
        ident_b = sb("ident_b", [P, P], BF16)
        mask_b = sb("mask_b", [P, 2, DEC], BF16)
        nsink = sb("nsink", [P, DEPTH, NH])
        a_exp = sb("a_exp", [P, DEPTH, DT])
        ctx_rows = sb("ctx_rows", [P, DEPTH, 4, NKV * HD])
        ckT = sb("ckT", [P, DEPTH, 2, P])
        h0T = sb("h0T", [P, DEPTH, 2, 2 * P])
        wr = sb("wr", [P, DEPTH, KD, NG + NE])
        small = sb("small", [P, 32])
        flag = sb("flag", [P, DEPTH], I32)

        def c_(name, n=P):
            return const[:, C_AT[name]:C_AT[name] + n]

        mix = ExitStack()
        with mix:
            row = sb("row", [P, TILES, 1024], c=mix)
            z = sb("z", [P, TILES, DS], c=mix)
            xbc = sb("xbc", [P, 6, TOK], c=mix)
            qkT = sb("qkT", [P, 6, TOK], c=mix)
            pT = sb("pT", [P, 3, 3 * P], c=mix)
            y = sb("y", [P, TILES, DS], c=mix)
            h0 = y.rearrange("p m n -> p (m n)")[:, 0:DEPTH * 512].rearrange(
                "p (l d j g n) -> p l d j g n", l=DEPTH, d=2, j=2, g=2)
            xs = sb("xs", [P, DS], c=mix)
            bro = sb("bro", [P, P], c=mix)
            gm = sb("gm", [P, 2, 2, P], c=mix)
            xd = sb("xd", [P, 2, SH, HD], c=mix)
            xdd = sb("xdd", [P, 2, SH, HD], c=mix)
            ud = sb("ud", [P, 2, SH, P], c=mix)
            mm = sb("mm", [P, 2, SH, P], c=mix)
            hin = sb("hin", [P, 2, 2 * P], c=mix)
            tmp = sb("tmp", [P, 3, DS], c=mix)
            stout = sb("stout", [P, 2, 4, HD], c=mix)
            dts = sb("dts", [P, TILES, DT], c=mix)
            dav = sb("dav", [P, TILES, DT], c=mix)
            dtw = sb("dtw", [P, 6, TILES * DT], c=mix)
            ex = sb("ex", [P, TILES, 48], c=mix)
            att = sb("att", [P, 6, len(HEADS)], c=mix)
            nrm = sb("nrm", [P, 32], c=mix)
            probs = hT.rearrange("p c t -> p (c t)")[:, 0:4 * TOK].rearrange("p (b t) -> p b t", b=4)
            yx = sb("yx", [P, DS], c=mix)
            sq = row.rearrange("p m n -> p (m n)").rearrange("p (c t) -> p c t", c=KD)
        moe = ExitStack()
        with moe:
            h_hi = sb("h_hi", [P, TILES, KD, P], F32R, c=moe)
            h_lo = sb("h_lo", [P, TILES, KD, P], F32R, c=moe)
            sel = sb("sel", [P, TILES, NG, P], F32R, c=moe)
            selT = sb("selT", [P, NG, TOK], F32R, c=moe)
            xg = sb("xg", [P, KD, NG, P], c=moe)
            sg = sb("sg", [P, 2, FE], c=moe)
            lgT = sg.rearrange("p b f -> p (b f)")[0:NG + NE, 0:TOK]
            hid = sb("hid", [P, 2, FE], c=moe)
            hidT = sb("hidT", [P, 2, FE], F32R, c=moe)
            y_hi = sb("y_hi", [P, NG, D], F32R, c=moe)
            y_lo = sb("y_lo", [P, NG, D], F32R, c=moe)
            down_lo = (y_lo[:, NG - 1, :], y_hi[:, NG - 1, :])
            lg = sb("lg", [P, TILES, NG + NE], c=moe)
            rt = sb("rt", [P, 24, TILES, NG], c=moe)
            e16 = sb("e16", [P, TILES, NE], c=moe)
            cwg = sb("cwg", [P, NG, EPG], c=moe)
        psum = ctx.enter_context(nc.psum_tensor("psum", [P, 8, 512], F32))[:]

        bank_full = [sem(f"bank{b}_full") for b in range(8)]
        bank_read = [sem(f"bank{b}_read") for b in range(8)]
        ring_full = [sem(f"ring{b}_full") for b in range(RING)]
        pieces_used = sem("pieces_used")
        const_in, x_in, c_in, prow_in, tab_in, cache_in, wr_in = (sem(n) for n in (
            "const_in", "x_in", "c_in", "prow_in", "tab_in", "cache_in", "wr_in"))
        dve_step, act_step, pool_step = (sem(n) for n in ("dve_step", "act_step", "pool_step"))
        out_sem = [sem(f"out{i}") for i in range(6)]
        y_out = sem("y_out")
        cols_ready, siluc_ready = sem("cols_ready"), sem("siluc_ready")
        setup_act, setup_dve = sem("setup_act"), sem("setup_dve")
        sig, per = {}, {}
        dve_steps, act_steps, pool_steps = counter(), counter(), counter()
        for name, n in (
                ("sq", 8), ("rstd", 2), ("h", 16), ("xbc_silu", 6), ("dt_na", 1), ("dt_u", 1),
                ("dt_r", 1), ("da", 1), ("bss", 3), ("brs", 3), ("prep", 3), ("ud", 3), ("xd", 3), ("yx", 3),
                ("seg", 12), ("zs", 1), ("nb", 24), ("es", 12), ("yz", 1), ("yrs", 1), ("yn", 1),
                ("flag", 1), ("ge0", 1), ("ge", 1), ("ed0", 1), ("ed", 1), ("goh", 1), ("cw", 1), ("hhi", 6),
                ("sel", 1), ("sgl", NE), ("yhi", 2 * NG), ("whi", 2 * NE), ("wlo", NE), ("hthi", NE)):
            sig[name], per[name] = sem(name), n

        more_full = [[sem(f"more{l}_bank{b}_full") for b in range(8)] for l in range(DEPTH)]
        more_read = [[sem(f"more{l}_bank{b}_read") for b in range(8)] for l in range(DEPTH)]
        more_ring = [[sem(f"more{l}_ring{b}_full") for b in range(RING)] for l in range(DEPTH)]
        more_used = [sem(f"more{l}_pieces_used") for l in range(DEPTH)]
        more_sig = [{n: sem(f"more{l}_{n}") for n in ("sel", "sgl", "yhi", "whi", "wlo", "hthi")} for l in range(DEPTH)]

        block = ctx.enter_context(nc.Block())

        uses, read_at, fills, reads = {}, {}, [0] * 8, [0] * 8
        turn = [0]
        release, used_count = {}, [0]

        release, used_count = {}, counter()
        more_fills, more_reads = [[0] * 8 for _ in range(DEPTH)], [[0] * 8 for _ in range(DEPTH)]
        more_used_count = [counter() for _ in range(DEPTH)]

        def more(key):
            return key[0] in ("selT", "cwg", "xg", "gu", "hidT", "yg", "sc", "gate", "up", "down") and key[2] > 0

        def raised(name, l, p):
            return more_sig[l][name] if p else sig[name]

        def times(name, l, p, n):
            return (p - 1 if p else l) * per[name] + n

        def fill(key, b=None):
            if b is None:
                turn[0] = (turn[0] + 1) % 7
                b = turn[0]
            n_reads, n_fills = (more_reads[key[1]], more_fills[key[1]]) if more(key) else (reads, fills)
            before = n_reads[b]
            n_reads[b] += 1
            n_fills[b] += 1
            uses[key], read_at[key] = (b, n_fills[b]), n_reads[b]
            return read_sem(key), before

        def read_sem(key):
            return (more_read[key[1]] if more(key) else bank_read)[uses[key][0]]

        def full_sem(key):
            return (more_full[key[1]] if more(key) else bank_full)[uses[key][0]]

        def bank(key):
            return psum[:, uses[key][0], :]

        def filled(key):
            return full_sem(key), 1

        def full(key):
            return full_sem(key), uses[key][1]

        def was_read(key):
            return read_sem(key), 1

        def taken(key):
            return read_sem(key), read_at[key]

        def landed(key):
            n = piece_at[key]
            return (more_ring[key[1]] if more(key) else ring_full)[n % RING], 16 * (n // RING + 1)

        def slot(key):
            return ring[:, piece_at[key] % RING, :]

        def used(key):
            if more(key):
                release[key] = (more_used[key[1]], more_used_count[key[1]]())
            else:
                release[key] = (pieces_used, used_count())
            return release[key][0], 1

        def used_with(key, filling):
            release[key] = full(filling)

        def turn_probs(eng, copy, l, u):
            w = P if HEADS[u][0] == 0 else TOK
            key = ("turn", l, u)
            eng.wait_ge(*full(key))
            src = bank(key)
            if u >= 3:
                eng.wait_ge(*full(("values", l, u - 3)))
            copy(pT[:, u % 3, 0:w], src[:, 0:w]).then_inc(*was_read(key))

        def gathered(eng, copy, l, p, t):
            key = ("xg", l, p, t)
            eng.wait_ge(*full(key))
            src = bank(key)
            if p:
                eng.wait_ge(*full(("gu", l, p - 1, NE - 1)))
            copy(xg[:, t, :, :].rearrange("p g s -> p (g s)"), src).then_inc(*was_read(key))

        @block.tensor
        def _(pe):
            ident = c_("ident")

            def ada(l, t, k):
                key = ("ada", l, t)
                pe.wait_ge(*landed(("ada", l, t, k)))
                w = slot(("ada", l, t, k))
                if k == 0:
                    pe.wait_ge(*fill(key, 7))
                for q in range(4):
                    last = pe.matmul(psum[32 * q:32 * q + 32, 7, :], silu_c[:, k, :], w[:, q * 512:(q + 1) * 512],
                                     start=(k == 0), stop=(k == KD - 1), skip_group_check=True,
                                     tile_position=(0, 32 * q))
                if k == KD - 1:
                    last.then_inc(*filled(key))
                    used_with(("ada", l, t, k), key)
                else:
                    last.then_inc(*used(("ada", l, t, k)))

            def ada_turn(l, t):
                pe.wait_ge(*taken(("ada", l, t)))
                pe.wait_ge(*fill(("adaT", l, t), 7))
                for i in range(4):
                    last = pe.transpose(psum[:, 7, i * P:(i + 1) * P], ada_rows[:, i * P:(i + 1) * P], ident)
                last.then_inc(*filled(("adaT", l, t)))

            pe.wait_ge(const_in, 16)
            pe.wait_ge(x_in, 32)
            for c in range(KD):
                pe.wait_ge(*fill(("xin", c)))
                dst = bank(("xin", c))
                for m in range(TILES):
                    last = pe.transpose(dst[:, m * P:(m + 1) * P], row[:, m, c * P:(c + 1) * P], ident)
                last.then_inc(*filled(("xin", c)))
            pe.wait_ge(c_in, 16 * 3)
            pe.wait_ge(*fill(("ccol",)))
            pe.transpose(bank(("ccol",))[:, 0:24], prow[0:24, 2, :], ident[0:24, 0:24]).then_inc(*filled(("ccol",)))

            def sums(key, l, n, base):
                pe.wait_ge(*fill(key))
                dst = bank(key)
                for c in range(KD):
                    if c % 2 == 0:
                        pe.wait_ge(sig["sq"], base + c // 2 + 1)
                    last = pe.matmul(dst[:, 0:TOK], c_("ones"), sq[:, c, :], start=(c == 0), stop=(c == KD - 1))
                last.then_inc(*filled(key))

            pe.wait_ge(setup_dve, 1)
            sums(("ss", 0, 0), 0, 0, 0)
            pe.wait_ge(siluc_ready, 1)
            pe.wait_ge(prow_in, 16 * 6 * DEPTH)
            pe.wait_ge(*fill(("pcol",)))
            dst = bank(("pcol",))
            for i in range(DEPTH):
                last = pe.transpose(dst[:, i * N_PROW:(i + 1) * N_PROW], prow[0:N_PROW, i, :], ident[0:N_PROW, 0:N_PROW])
            last.then_inc(*filled(("pcol",)))
            for k in range(KD):
                ada(0, 0, k)
            ada_turn(0, 0)

            def moe(l, kind, arg):
                if kind == "select":
                    p = arg[0]
                    pe.wait_ge(raised("sel", l, p), times("sel", l, p, 1))
                    for g in range(NG):
                        pe.wait_ge(*fill(("selT", l, p, g)))
                        dst = bank(("selT", l, p, g))
                        for m in range(TILES):
                            last = pe.transpose(dst[:, m * P:(m + 1) * P], sel[:, m, g, :].bitcast(F32), ident)
                        last.then_inc(*filled(("selT", l, p, g)))
                    pe.wait_ge(sig["cw"], per["cw"] * l + 1)
                    pe.wait_ge(*fill(("cwg", l, p)))
                    dst = bank(("cwg", l, p))
                    for g in range(NG):
                        for m in range(TILES):
                            last = pe.matmul(dst[:, g * EPG:(g + 1) * EPG], sel[:, m, g, :].bitcast(F32),
                                             rt[:, 1, m, :], start=(m == 0), stop=(m == TILES - 1))
                    last.then_inc(*filled(("cwg", l, p)))
                elif kind == "gather":
                    p = arg[0]
                    for m in range(TILES):
                        for half in range(2):
                            pe.wait_ge(*taken(("hrow", l, m, half)))
                    for t in range(KD):
                        pe.wait_ge(*fill(("xg", l, p, t)))
                        dst = bank(("xg", l, p, t))
                        for i, src in enumerate((h_hi, h_lo)):
                            for m in range(TILES):
                                last = pe.matmul(dst[:, 0:NG * P], src[:, m, t, :],
                                                 sel[:, m, :, :].rearrange("p g s -> p (g s)"),
                                                 start=(i == 0 and m == 0), stop=(i == 1 and m == TILES - 1))
                        last.then_inc(*filled(("xg", l, p, t)))
                elif kind in ("gate_half", "gu"):
                    p, e = arg
                    g = e // EPG
                    i, name = (0, "gate") if kind == "gate_half" else (1, "up")
                    if e == 0 and i == 0:
                        for t in range(KD):
                            pe.wait_ge(*taken(("xg", l, p, t)))
                    pe.wait_ge(*landed((name, l, p, e)))
                    w = slot((name, l, p, e)).rearrange("p (t f) -> p t f", t=KD)
                    if i == 0:
                        pe.wait_ge(*fill(("gu", l, p, e), 4 + e % 2))
                    dst = bank(("gu", l, p, e))
                    for t in range(KD):
                        last = pe.matmul(dst[:, i * FE:(i + 1) * FE], xg[:, t, g, :], w[:, t, :],
                                         start=(t == 0), stop=(t == KD - 1))
                    if i == 0:
                        last.then_inc(*used((name, l, p, e)))
                    else:
                        last.then_inc(*filled(("gu", l, p, e)))
                        used_with((name, l, p, e), ("gu", l, p, e))
                elif kind == "turn_hid":
                    p, e = arg
                    pe.wait_ge(*taken(("gu", l, p, e)))
                    pe.wait_ge(*fill(("hidT", l, p, e), 6))
                    dst = bank(("hidT", l, p, e))
                    for f in range(2):
                        last = pe.transpose(dst[:, f * P:(f + 1) * P], hid[:, e % 2, f * P:(f + 1) * P], ident)
                    last.then_inc(*filled(("hidT", l, p, e)))
                elif kind == "down":
                    p, e = arg
                    g = e // EPG
                    pe.wait_ge(*taken(("hidT", l, p, e)))
                    pe.wait_ge(*landed(("down", l, p, e)))
                    pe.wait_ge(raised("wlo", l, p), times("wlo", l, p, e + 1))
                    w_hi = (down_hi[:, 0:D], down_hi[:, D:])
                    products = [(x[:, e % 2, f * P:(f + 1) * P], w[f]) for x, w in
                                ((hidT, w_hi), (hidT, down_lo), (hidT_lo, w_hi)) for f in range(2)]
                    for half in range(2):
                        b = 2 * (g % 2) + half
                        if e % EPG == 0:
                            pe.wait_ge(*fill(("yg", l, p, g, half), b))
                        for i, (x, w) in enumerate(products):
                            last = pe.matmul(psum[:, b, :], x, w[:, half * 512:(half + 1) * 512],
                                             start=(e % EPG == 0 and i == 0),
                                             stop=(e % EPG == EPG - 1 and i == len(products) - 1))
                        if e % EPG == EPG - 1:
                            last.then_inc(*filled(("yg", l, p, g, half)))
                    if e % EPG == EPG - 1:
                        used_with(("down", l, p, e), ("yg", l, p, g, 1))
                    else:
                        last.then_inc(*used(("down", l, p, e)))
                elif kind == "scatter":
                    p = arg[0]
                    for g in range(NG):
                        pe.wait_ge(*taken(("selT", l, p, g)))
                        for half in range(2):
                            pe.wait_ge(*taken(("yg", l, p, g, half)))
                    for c in range(KD):
                        pe.wait_ge(*fill(("sc", l, p, c)))
                        dst = bank(("sc", l, p, c))
                        for i, src in enumerate((y_hi, y_lo)):
                            for g in range(NG):
                                last = pe.matmul(dst[:, 0:TOK], src[:, g, c * P:(c + 1) * P], selT[:, g, :],
                                                 start=(i == 0 and g == 0), stop=(i == 1 and g == NG - 1))
                        last.then_inc(*filled(("sc", l, p, c)))

            for l in range(DEPTH):
                for step in STEPS[l]:
                    kind, arg = step[0], step[1:]
                    if kind == "norm":
                        n = arg[0]
                        if l or n:
                            sums(("ss", l, n), l, n, (2 * l + n) * 4)
                    elif kind == "caches":
                        pe.wait_ge(cache_in, 16 * 12 * DEPTH)
                        for lc in range(DEPTH):
                            pe.wait_ge(*fill(("ck", lc)))
                            dst = bank(("ck", lc))
                            for t in range(2):
                                last = pe.transpose(dst[:, t * P:(t + 1) * P], ctx_rows[:, lc, t, :], ident)
                            last.then_inc(*filled(("ck", lc)))
                            pe.wait_ge(*fill(("h0", lc)))
                            dst = bank(("h0", lc))
                            for d in range(2):
                                for j in range(2):
                                    last = pe.transpose(dst[:, d * 256 + j * P:d * 256 + (j + 1) * P],
                                                        h0[:, lc, d, j, :, :].rearrange("p g n -> p (g n)"), ident)
                            last.then_inc(*filled(("h0", lc)))
                    elif kind == "ada":
                        ada(*arg)
                    elif kind == "ada_turn":
                        ada_turn(*arg)
                    elif kind == "xbc":
                        for c in range(6):
                            pe.wait_ge(*fill(("xbc", l, c)))
                        dsts = [bank(("xbc", l, c)) for c in range(6)]
                        pe.wait_ge(*fill(("dt", l)))
                        dtd = bank(("dt", l))
                        for i in range(KD // 2):
                            pe.wait_ge(*landed(("xbc", l, i)))
                            w = slot(("xbc", l, i))[:, 0:2 * (XBC + DT)].rearrange("p (k n) -> p k n", k=2)
                            for kk in range(2):
                                k = 2 * i + kk
                                pe.wait_ge(sig["h"], per["h"] * l + k + 1)
                                for m in range(TILES):
                                    last = pe.matmul(dtd[:, m * DT:(m + 1) * DT], hT[:, k, m * P:(m + 1) * P],
                                                     w[:, kk, XBC:XBC + DT], start=(k == 0 and m == 0),
                                                     stop=(k == KD - 1), skip_group_check=True)
                                if k == KD - 1:
                                    last.then_inc(*filled(("dt", l)))
                                for c in range(6):
                                    last = pe.matmul(dsts[c][:, 0:TOK], w[:, kk, c * P:(c + 1) * P], hT[:, k, :],
                                                     start=(k == 0), stop=(k == KD - 1))
                                    if k == KD - 1:
                                        last.then_inc(*filled(("xbc", l, c)))
                            if i < KD // 2 - 1:
                                last.then_inc(*used(("xbc", l, i)))
                            else:
                                used_with(("xbc", l, i), ("xbc", l, 5))
                    elif kind == "rows":
                        m = arg[0]
                        for g in range(3):
                            pe.wait_ge(*fill(("row", l, m, g)))
                            dst = bank(("row", l, m, g))
                            for k in range(KD):
                                pe.wait_ge(*landed(("win", l, k)))
                                w = slot(("win", l, k))
                                last = pe.matmul(dst[:, 0:512], hT[:, k, m * P:(m + 1) * P],
                                                 w[:, g * 512:(g + 1) * 512], start=(k == 0), stop=(k == KD - 1))
                            last.then_inc(*filled(("row", l, m, g)))
                    elif kind == "rows_last":
                        m = TILES - 1
                        for g in range(3):
                            pe.wait_ge(*fill(("row", l, m, g)))
                        dsts = [bank(("row", l, m, g)) for g in range(3)]
                        for k in range(KD):
                            pe.wait_ge(*landed(("win", l, k)))
                            w = slot(("win", l, k))
                            for g in range(3):
                                last = pe.matmul(dsts[g][:, 0:512], hT[:, k, m * P:(m + 1) * P],
                                                 w[:, g * 512:(g + 1) * 512], start=(k == 0), stop=(k == KD - 1))
                                if k == KD - 1:
                                    last.then_inc(*filled(("row", l, m, g)))
                            if k < KD - 1:
                                last.then_inc(*used(("win", l, k)))
                            else:
                                used_with(("win", l, k), ("row", l, m, 2))
                    elif kind == "turn_qk":
                        m = arg[0]
                        pe.wait_ge(sig["prep"], per["prep"] * l + m + 1)
                        pe.wait_ge(*taken(("row", l, m, 0)))
                        pe.wait_ge(*taken(("row", l, m, 1)))
                        for t in range(2):
                            pe.wait_ge(*fill(("qkT", l, m, t)))
                            dst = bank(("qkT", l, m, t))
                            for i in range(3):
                                at = t * OFF_B + i * P
                                last = pe.transpose(dst[:, i * P:(i + 1) * P], row[:, m, at:at + P], ident)
                            last.then_inc(*filled(("qkT", l, m, t)))
                    elif kind == "ssm_in":
                        m = arg[0]
                        tok = slice(m * P, (m + 1) * P)
                        pe.wait_ge(sig["xbc_silu"], per["xbc_silu"] * l + 6)
                        pe.wait_ge(*fill(("xs", l, m)))
                        dst = bank(("xs", l, m))
                        for c in range(4):
                            last = pe.transpose(dst[:, c * P:(c + 1) * P], xbc[:, c, tok], ident)
                        last.then_inc(*filled(("xs", l, m)))
                        pe.wait_ge(*fill(("bg", l, m)))
                        dst = bank(("bg", l, m))
                        pe.transpose(dst[:, 0:P], xbc[:, 4, tok], ident)
                        for g in range(2):
                            if g:
                                pe.wait_ge(*fill(("bg1", l, m)))
                                dst = bank(("bg1", l, m))
                            last = pe.matmul(dst[:, P:2 * P], xbc[g * 64:g * 64 + 64, 4, tok],
                                             xbc[g * 64:g * 64 + 64, 5, tok], start=True, stop=True)
                            last.then_inc(*filled(("bg1" if g else "bg", l, m)))
                        pe.wait_ge(sig["da"], per["da"] * l + 1)
                        pe.wait_ge(*fill(("cum", l, m)))
                        dst = bank(("cum", l, m))
                        for i, (tri_f, tri_b) in enumerate((("incl_f", "incl_b"), ("after", "before"))):
                            pe.matmul(dst[:, 16 * i:16 * i + 8], c_(tri_f), dav[:, m, 0:8], start=True, stop=True)
                            pe.matmul(dst[:, 16 * i + 8:16 * i + 16], c_(tri_b), dav[:, m, 8:16], start=True, stop=True)
                        last = pe.matmul(dst[:, 32:48], c_("ones"), dav[:, m, :], start=True, stop=True)
                        last.then_inc(*filled(("cum", l, m)))
                    elif kind == "seg":
                        m = arg[0]
                        pe.wait_ge(sig["ud"], per["ud"] * l + m + 1)
                        for d, tri in enumerate(("after", "before")):
                            for g in range(2):
                                pe.wait_ge(*fill(("seg", l, m, d, g)))
                                dst = bank(("seg", l, m, d, g))
                                last = pe.matmul(dst[:, 0:512], c_(tri),
                                                 ud[:, d, 4 * g:4 * g + 4, :].rearrange("p h t -> p (h t)"),
                                                 start=True, stop=True)
                                last.then_inc(*filled(("seg", l, m, d, g)))
                    elif kind == "ssm_y":
                        m = arg[0]
                        for d in range(2):
                            for g in range(2):
                                pe.wait_ge(*taken(("seg", l, m, d, g)))
                        pe.wait_ge(*taken(("bg", l, m)))
                        pe.wait_ge(*taken(("bg1", l, m)))
                        pe.wait_ge(sig["xd"], per["xd"] * l + m + 1)
                        pe.wait_ge(*fill(("ydiag", l, m)))
                        dst = bank(("ydiag", l, m))
                        for h in range(SH):
                            for d in range(2):
                                last = pe.matmul(dst[:, h * HD:(h + 1) * HD], mm[:, d, h, :], xd[:, d, h, :],
                                                 start=(d == 0), stop=(d == 1))
                        last.then_inc(*filled(("ydiag", l, m)))
                        pe.wait_ge(*fill(("state", l, m)))
                        dst = bank(("state", l, m))
                        if m == 0:
                            for d in range(2):
                                for pr in range(4):
                                    g = pr // 2
                                    last = pe.matmul(dst[:, d * 256 + pr * HD:d * 256 + (pr + 1) * HD],
                                                     xdd[:, d, 2 * pr:2 * pr + 2, :].rearrange("p h n -> p (h n)"),
                                                     bro[:, g * 64:g * 64 + 64], start=True, stop=True)
                        else:
                            d = m - 1
                            for g in range(2):
                                last = pe.matmul(dst[g * 64:g * 64 + 64, 0:256], bro[:, g * 64:g * 64 + 64],
                                                 xdd[:, d, 4 * g:4 * g + 4, :].rearrange("p h n -> p (h n)"),
                                                 start=True, stop=True)
                        last.then_inc(*filled(("state", l, m)))
                    elif kind == "ssm_off":
                        m = arg[0]
                        pe.wait_ge(*taken(("state", l, 1)))
                        pe.wait_ge(*taken(("state", l, 2)))
                        for g in range(2):
                            pe.wait_ge(*fill(("yoff", l, m, g)))
                            dst = bank(("yoff", l, m, g))
                            for d in range(2):
                                src = h0T[:, l, d, :] if (m, d) in ((1, 0), (2, 1)) else hin[:, d, :]
                                last = pe.matmul(dst[:, d * 256:(d + 1) * 256],
                                                 xbc[g * 64:g * 64 + 64, 5, m * P:(m + 1) * P],
                                                 src[g * 64:g * 64 + 64, :], start=True, stop=True)
                            last.then_inc(*filled(("yoff", l, m, g)))
                    elif kind == "scores":
                        u = arg[0]
                        m, t, h = HEADS[u]
                        kv, i = h // 2, h % 2
                        part = slice(kv * 64, kv * 64 + 64)
                        if u == 0:
                            for mq in range(TILES):
                                for tq in range(2):
                                    pe.wait_ge(*taken(("qkT", l, mq, tq)))
                        pe.wait_ge(*fill(("scores", l, u)))
                        dst = bank(("scores", l, u))
                        q = qkT[part, 3 * t + i, m * P:(m + 1) * P]
                        if m == 0:
                            last = pe.matmul(dst[:, 0:P], q, qkT[part, 3 * t + 2, 0:P], start=True, stop=True)
                        else:
                            pe.matmul(dst[:, 0:DEC], q, qkT[part, 3 * t + 2, P:TOK], start=True, stop=(t == 1))
                            if t == 0:
                                pe.matmul(dst[:, 0:DEC], ident_b, mask_b[:, m - 1, :], start=False, stop=True)
                            last = pe.matmul(dst[:, DEC:DEC + P], q, ckT[part, l, t, :], start=True, stop=True)
                        last.then_inc(*filled(("scores", l, u)))
                    elif kind == "turn":
                        u = arg[0]
                        m = HEADS[u][0]
                        pe.wait_ge(*taken(("scores", l, u)))
                        pe.wait_ge(*fill(("turn", l, u)))
                        dst = bank(("turn", l, u))
                        for c in range(1 if m == 0 else 3):
                            last = pe.transpose(dst[:, c * P:(c + 1) * P], probs[:, u % 4, c * P:(c + 1) * P], ident)
                        last.then_inc(*filled(("turn", l, u)))
                    elif kind == "values":
                        u = arg[0]
                        m, t, h = HEADS[u]
                        v = slice(t * OFF_B + 384 + (h // 2) * HD, t * OFF_B + 384 + (h // 2) * HD + HD)
                        pe.wait_ge(*taken(("turn", l, u)))
                        pe.wait_ge(*fill(("values", l, u)))
                        dst = bank(("values", l, u))
                        srcs = [row[:, 0, v]] if m == 0 else [row[:, 1, v], row[:, 2, v],
                                                              ctx_rows[:, l, 2 + t, (h // 2) * HD:(h // 2) * HD + HD]]
                        for c, vv in enumerate(srcs):
                            last = pe.matmul(dst[:, 0:HD], pT[:, u % 3, c * P:(c + 1) * P], vv,
                                             start=(c == 0), stop=(c == len(srcs) - 1))
                        last.then_inc(*filled(("values", l, u)))
                    elif kind == "turn_mix":
                        for u in range(len(HEADS) - 7, len(HEADS)):
                            pe.wait_ge(*taken(("values", l, u)))
                        for c in range(KD):
                            if c == 4:
                                pe.wait_ge(sig["yn"], per["yn"] * l + 1)
                            pe.wait_ge(*fill(("mix", l, c)))
                            dst = bank(("mix", l, c))
                            for m in range(TILES):
                                src = row[:, m, (0, P, OFF_B, OFF_B + P)[c]:(0, P, OFF_B, OFF_B + P)[c] + P] if c < 4 \
                                    else y[:, m, (c - 4) * P:(c - 3) * P]
                                last = pe.transpose(dst[:, m * P:(m + 1) * P], src, ident)
                            last.then_inc(*filled(("mix", l, c)))
                    elif kind == "wout":
                        for c in range(KD):
                            pe.wait_ge(*fill(("wout", l, c)))
                            dst = bank(("wout", l, c))
                            for k in range(KD):
                                if c == 0:
                                    pe.wait_ge(*taken(("mix", l, k)))
                                pe.wait_ge(*landed(("wout", l, k // 2)))
                                w = slot(("wout", l, k // 2))
                                last = pe.matmul(dst[:, 0:TOK], w[:, (k % 2) * D + c * P:(k % 2) * D + (c + 1) * P],
                                                 hT[:, k, :], start=(k == 0), stop=(k == KD - 1))
                                if c == KD - 1 and k % 2 and k < KD - 1:
                                    last.then_inc(*used(("wout", l, k // 2)))
                            last.then_inc(*filled(("wout", l, c)))
                        used_with(("wout", l, 3), ("wout", l, KD - 1))
                    elif kind == "router":
                        n = NG + NE
                        pe.wait_ge(wr_in, 16 * 2 * DEPTH)
                        pe.wait_ge(*fill(("logitsT", l)))
                        dst = bank(("logitsT", l))
                        for k in range(KD):
                            pe.wait_ge(sig["h"], per["h"] * l + KD + k + 1)
                            last = pe.matmul(dst[0:n, 0:TOK], wr[:, l, k, :], hT[:, k, :],
                                             start=(k == 0), stop=(k == KD - 1))
                        last.then_inc(*filled(("logitsT", l)))
                        pe.wait_ge(*taken(("logitsT", l)))
                        pe.wait_ge(*fill(("logits", l)))
                        dst = bank(("logits", l))
                        for m in range(TILES):
                            last = pe.transpose(dst[:, m * n:(m + 1) * n], lgT[:, m * P:(m + 1) * P],
                                                ident[0:n, 0:n])
                        last.then_inc(*filled(("logits", l)))
                    elif kind == "hrow":
                        for m in range(TILES):
                            for half in range(2):
                                pe.wait_ge(*fill(("hrow", l, m, half)))
                                dst = bank(("hrow", l, m, half))
                                for j in range(4):
                                    last = pe.transpose(dst[:, j * P:(j + 1) * P],
                                                        hT[:, 4 * half + j, m * P:(m + 1) * P], ident)
                                last.then_inc(*filled(("hrow", l, m, half)))
                    elif kind == "rank":
                        pe.wait_ge(sig["goh"], per["goh"] * l + 1)
                        pe.wait_ge(*fill(("rank", l)))
                        dst = bank(("rank", l))
                        for m in range(TILES):
                            for mm_ in range(m + 1):
                                last = pe.matmul(dst[:, m * NG:(m + 1) * NG], c_("before" if mm_ == m else "ones"),
                                                 rt[:, 0, mm_, :], start=(mm_ == 0), stop=(mm_ == m))
                        for m in range(TILES):
                            last = pe.matmul(dst[:, TILES * NG:(TILES + 1) * NG], c_("ones"), rt[:, 0, m, :],
                                             start=(m == 0), stop=(m == TILES - 1))
                        last.then_inc(*filled(("rank", l)))
                    elif kind == "more":
                        pe.wait_ge(sig["flag"], l + 1)
                        over = pe.value_load(flag[0:1, l:l + 1], min_val=0, max_val=1)
                        with pe.If(over != 0):
                            for b in range(8):
                                pe.wait_ge(bank_read[b], reads[b])
                            for kind, *arg in more_steps():
                                moe(l, kind, arg)
                            for b in range(8):
                                pe.wait_ge(more_read[l][b], more_reads[l][b])
                    else:
                        moe(l, kind, arg)
            sums(("ss", DEPTH, 0), DEPTH, 0, 2 * DEPTH * 4)
            for m in range(TILES):
                for half in range(2):
                    if m == 0 and half == 0:
                        pe.wait_ge(sig["h"], 16 * DEPTH + 8)
                    pe.wait_ge(*fill(("out", m, half)))
                    dst = bank(("out", m, half))
                    for j in range(4):
                        last = pe.transpose(dst[:, j * P:(j + 1) * P], hT[:, 4 * half + j, m * P:(m + 1) * P], ident)
                    last.then_inc(*filled(("out", m, half)))

        @block.sync
        def _(sp):
            for i, src in enumerate((a["final_norm_g"], a["c_ctx"], a["c"][0])):
                sp.dma_start(prow[8 * i:8 * i + 8, 2, :], src.rearrange("(r p) -> r p", p=P)).then_inc(c_in, 16)
            sp.dma_start(const, a["const"]).then_inc(const_in, 16)
            sp.dma_start(row[:, 0, :], a["x_prompt"][0]).then_inc(x_in, 16)
            sp.dma_start(row[:, 1:3, :], a["x_sample"][0].rearrange("(m p) d -> p m d", p=P)).then_inc(x_in, 16)
            def small_parameters():
                for l in range(DEPTH):
                    for name, at, n in (("dt_bias", T_DTB, 16), ("a_log", T_AL, 16), ("d_skip", T_DSK, 8),
                                        ("a_sink", T_SINK, 4), ("b_router_group", T_BG, 4), ("b_router_expert", T_BE, 16)):
                        src = a[name][l]
                        if len(src.shape) == 2:
                            src = src.rearrange("a b -> (a b)")
                        sp.dma_start(tab[:, l, at:at + n], src.partition_broadcast(P)).then_inc(tab_in, 16)
                    for name, at, n in (("q_norm_g", T_GQK, 4), ("k_norm_g", T_GQK + 4 * HD, 2)):
                        sp.dma_start(tab[:, l, at:at + n * HD].rearrange("p (a b) -> p a b", a=n),
                                      a[name][l].unsqueeze(0).unsqueeze(0).to_broadcast((P, n, HD))).then_inc(tab_in, 16)
                    for i, name in enumerate(("cache_a_k", "cache_b_k", "cache_a_v", "cache_b_v")):
                        sp.dma_start(ctx_rows[:, l, i, :], a[name][0, l].rearrange("s k d -> s (k d)"))\
                            .then_inc(cache_in, 16)
                    for d, name in enumerate(("state_ssm_fwd", "state_ssm_bwd")):
                        for j in range(2):
                            for g in range(2):
                                sp.dma_start(h0[:, l, d, j, g, :],
                                              a[name][0, l, 4 * g + 2 * j:4 * g + 2 * j + 2].rearrange("h p n -> (h p) n"))\
                                    .then_inc(cache_in, 16)
                    sp.dma_start(wr[:, l, :, 0:NG], a["w_router_group"][l].rearrange("(k p) n -> p k n", p=P))\
                        .then_inc(wr_in, 16)
                    sp.dma_start(wr[:, l, :, NG:], a["w_router_expert"][l].rearrange("(k p) n -> p k n", p=P))\
                        .then_inc(wr_in, 16)

            def load(key, full_sem, n):
                dst = ring[:, n % RING, :]
                kind, l, at = key[0], key[1], key[2:]
                if kind == "ada":
                    t, k = at
                    src = a["w_ada"][l, k * P:(k + 1) * P, t * PIECE:(t + 1) * PIECE]
                elif kind == "xbc":
                    src = a["w_in"][l, 2 * at[0] * P:2 * (at[0] + 1) * P, OFF_XBC:D_IN].rearrange(
                        "(k p) n -> p k n", p=P)
                    dst = dst[:, 0:2 * (XBC + DT)].rearrange("p (k n) -> p k n", k=2)
                elif kind == "win":
                    src, dst = a["w_in"][l, at[0] * P:(at[0] + 1) * P, 0:OFF_XBC], dst[:, 0:OFF_XBC]
                elif kind == "wout":
                    src = a["w_out"][l, 2 * at[0] * P:2 * (at[0] + 1) * P, :].rearrange("(k p) n -> p k n", p=P)
                    dst = dst.rearrange("p (k n) -> p k n", k=2)
                elif kind == "down":
                    src = a["w_down"][l, at[1]].rearrange("(f p) n -> p f n", p=P)
                    dst = dst.rearrange("p (f n) -> p f n", f=2)
                else:
                    src = a["w_" + kind][l, at[1]].rearrange("(p t) f -> p (t f)", t=KD)
                sp.dma_start(dst, src).then_inc(full_sem, 16)

            for n, key in enumerate(pieces):
                if n == RING:
                    small_parameters()
                if n >= RING:
                    sp.wait_ge(*release[pieces[n - RING]])
                load(key, ring_full[n % RING], n)
                l = key[1]
                if key != ("down", l, 0, NE - 1):
                    continue
                sp.wait_ge(sig["flag"], l + 1)
                over = sp.value_load(flag[0:1, l:l + 1], min_val=0, max_val=1)
                with sp.If(over != 0):
                    for former in pieces[n - RING + 1:n + 1]:
                        sp.wait_ge(*release[former])
                    for i, extra in enumerate(more_pieces):
                        if i >= RING:
                            sp.wait_ge(*release[(more_pieces[i - RING][0], l, *more_pieces[i - RING][1:])])
                        load((extra[0], l, *extra[1:]), more_ring[l][i % RING], i)
                    for extra in more_pieces[-RING:]:
                        sp.wait_ge(*release[(extra[0], l, *extra[1:])])
            for m in range(TILES):
                for half in range(2):
                    sp.wait_ge(*taken(("out", m, half)))
                dst = a_out[0][0] if m == 0 else a_out[1][0, (m - 1) * P:m * P, :]
                sp.dma_start(dst, row[:, m, :]).then_inc(y_out, 16)
            sp.wait_ge(y_out, 16 * TILES)
            for s in out_sem:
                sp.wait_ge(s, 16 * DEPTH)

        @block.scalar
        def _(act):

            for l in range(DEPTH):
                for name, r, n in (("norm1_g", R_N1, 8), ("norm2_g", R_N2, 8), ("b_ada", R_BADA, 48),
                                   ("conv_b", R_CB, 6), ("ssm_norm_g", R_SG, 4)):
                    act.dma_start(prow[r:r + n, l, :], a[name][l].rearrange("(r p) -> r p", p=P)).then_inc(prow_in, 16)
                act.dma_start(prow[R_CW:R_CW + 18, l, :],
                              a["conv_w"][l].rearrange("t (r p) -> (t r) p", p=P)).then_inc(prow_in, 16)
            act.wait_ge(cols_ready, 1)
            act.activation(small[:, 0:16], pcol[:, 2 * N_PROW + 8:2 * N_PROW + 24], ACT.Exp, scale=-1.0)\
                .then_inc(setup_act, 1)

            def ada(l, t):
                key = ("ada", l, t)
                act.wait_ge(*full(key))
                src = bank(key)
                act.copy(ada_rows, src).then_inc(*was_read(key))

            def norm(l, n):
                if not (l or n):
                    act.wait_ge(*taken(("xin", KD - 1)))
                if n:
                    for s in out_sem:
                        act.wait_ge(s, 16 * (l + 1))
                for j in range(4):
                    for c in (2 * j, 2 * j + 1):
                        act.wait_ge(*taken(("xin", c) if not (l or n) else ("wout", l, c) if n else ("sc", l - 1, 0, c)))
                    ins = act.activation(sq[:, 2 * j:2 * j + 2, :], xT[:, 2 * j:2 * j + 2, :], ACT.Square)
                    ins.then_inc(sig["sq"], 1)
                key = ("ss", l, n)
                act.wait_ge(*full(key))
                src = bank(key)
                act.activation(src[:, 0:TOK], src[:, 0:TOK], ACT.Ln, bias=eps_col, scale=1.0 / D).then_inc(act_step, 1)
                act.wait_ge(act_step, act_steps())
                act.activation(src[:, 0:TOK], src[:, 0:TOK], ACT.Exp, scale=-0.5).then_inc(sig["rstd"], 1)

            act.wait_ge(setup_dve, 1)
            def moe(l, kind, arg):
                if kind == "select":
                    p = arg[0]
                    if p:
                        act.wait_ge(*full(("sc", l, p - 1, KD - 1)))
                    for g in range(NG):
                        key = ("selT", l, p, g)
                        act.wait_ge(*full(key))
                        src = bank(key)
                        act.copy(selT[:, g, :], src[:, 0:TOK]).then_inc(*was_read(key))
                elif kind == "gather":
                    p = arg[0]
                    for t in range(0, KD, 2):
                        gathered(act, act.copy, l, p, t)
                elif kind == "gu":
                    p, e = arg
                    act.wait_ge(*full(("gu", l, p, e)))
                    src = bank(("gu", l, p, e))
                    if e >= 2:
                        act.wait_ge(*taken(("gu", l, p, e - 2)))
                    act.activation(sg[:, e % 2, :], src[:, 0:FE], ACT.Silu).then_inc(raised("sgl", l, p), 1)
                elif kind == "split":
                    p, e = arg
                    act.wait_ge(*landed(("down", l, p, e)))
                    if e:
                        act.wait_ge(*release[("down", l, p, e - 1)])
                    elif p:
                        act.wait_ge(*full(("sc", l, p - 1, KD - 1)))
                    else:
                        act.wait_ge(*full(("hrow", l, TILES - 1, 1)))
                    for half in range(2):
                        part = slice(half * D, (half + 1) * D)
                        act.copy(down_hi[:, part], slot(("down", l, p, e))[:, part]).then_inc(raised("whi", l, p), 1)
                elif kind == "turn_hid":
                    p, e = arg
                    key = ("hidT", l, p, e)
                    act.wait_ge(*full(key))
                    src = bank(key)
                    act.copy(hidT[:, e % 2, :], src[:, 0:2 * P]).then_inc(raised("hthi", l, p), 1)
                elif kind == "down":
                    p, e = arg
                    if e % EPG == EPG - 1:
                        g = e // EPG
                        for half in range(2):
                            act.wait_ge(*full(("yg", l, p, g, half)))
                            src = bank(("yg", l, p, g, half))
                            act.copy(y_hi[:, g, half * 512:(half + 1) * 512], src).then_inc(raised("yhi", l, p), 1)

            for l in range(DEPTH):
                for step in STEPS[l]:
                    kind, arg = step[0], step[1:]
                    if kind == "norm":
                        norm(l, arg[0])
                        if not (l or arg[0]):
                            ada(0, 0)
                    elif kind == "ada" and arg[2] == KD - 1:
                        ada(arg[0], arg[1])
                    elif kind == "xbc":
                        if l == 0:
                            act.wait_ge(tab_in, 16 * 8 * DEPTH)
                            act.activation(a_exp, tab[:, :, T_AL:T_AL + DT], ACT.Exp).then_inc(setup_act, 1)
                        for c in range(6):
                            act.wait_ge(*taken(("xbc", l, c)))
                            act.activation(xbc[:, c, :], xbc[:, c, :], ACT.Silu).then_inc(sig["xbc_silu"], 1)
                        act.wait_ge(sig["dt_na"], per["dt_na"] * l + 1)
                        ins = act.activation(dtw[:, 1, :], dtw[:, 1, :], ACT.Exp)
                        ins.then_inc(sig["dt_u"], 1)
                        act.wait_ge(sig["dt_u"], per["dt_u"] * l + 1)
                        act.activation(dtw[:, 2, :], dtw[:, 1, :], ACT.Ln, bias=one_col).then_inc(sig["dt_r"], 1)
                    elif kind in ("rows", "rows_last"):
                        m = arg[0] if arg else TILES - 1
                        for g in range(3):
                            key = ("row", l, m, g)
                            act.wait_ge(*full(key))
                            src = bank(key)
                            if g == 2:
                                act.copy(z[:, m, :], src).then_inc(*was_read(key))
                                continue
                            act.copy(row[:, m, g * 512:g * 512 + 256].rearrange("p (b a d) -> p a b d", a=2, b=2),
                                     src[:, 0:256].rearrange("p (a b d) -> p a b d", a=2, b=2))
                            act.copy(row[:, m, g * 512 + 256:(g + 1) * 512], src[:, 256:512]).then_inc(*was_read(key))
                    elif kind == "prep":
                        m = arg[0]
                        act.wait_ge(sig["bss"], per["bss"] * l + m + 1)
                        act.activation(nrm[:, 8:14], nrm[:, 0:6], ACT.Ln, bias=eps_col, scale=1.0 / HD).then_inc(act_step, 1)
                        act.wait_ge(act_step, act_steps())
                        act.activation(nrm[:, 16:22], nrm[:, 8:14], ACT.Exp, scale=-0.5).then_inc(sig["brs"], 1)
                        if m == 0:
                            act.wait_ge(sig["prep"], per["prep"] * l + 1)
                            for i, c0 in enumerate((256, 384, OFF_B + 256, OFF_B + 384)):
                                act.dma_start(a_out[2 + i][0, l].rearrange("s k d -> s (k d)"), row[:, 0, c0:c0 + P])\
                                    .then_inc(out_sem[i], 16)
                    elif kind == "turn_qk":
                        m = arg[0]
                        for t in range(2):
                            key = ("qkT", l, m, t)
                            act.wait_ge(*full(key))
                            src = bank(key)[:, 0:3 * P].rearrange("p (c t) -> p c t", c=3)
                            act.copy(qkT[:, 3 * t:3 * t + 3, m * P:(m + 1) * P], src).then_inc(*was_read(key))
                    elif kind == "ssm_in":
                        m = arg[0]
                        key = ("xs", l, m)
                        act.wait_ge(*full(key))
                        src = bank(key)
                        if m:
                            act.wait_ge(sig["xd"], per["xd"] * l + m)
                        act.copy(xs, src).then_inc(*was_read(key))
                        key = ("cum", l, m)
                        act.wait_ge(*full(key))
                        src = bank(key)
                        ins = act.activation(ex[:, m, :], src[:, 0:48], ACT.Exp)
                        ins.then_inc(*was_read(key))
                    elif kind == "seg":
                        m = arg[0]
                        for d in range(2):
                            for g in range(2):
                                act.wait_ge(*full(("seg", l, m, d, g)))
                                src = bank(("seg", l, m, d, g))
                                act.activation(src, src, ACT.Exp).then_inc(sig["seg"], 1)
                    elif kind == "ssm_y":
                        if arg[0] == 0:
                            key = ("state", l, 0)
                            act.wait_ge(*full(key))
                            src = bank(key)
                            ins = act.copy(stout.rearrange("p a b n -> p (a b n)"), src)
                            ins.then_inc(*was_read(key))
                            act.wait_ge(*taken(key))
                            for d in range(2):
                                act.dma_start(a_out[6 + d][0, l].rearrange("(r h) p n -> (h p) r n", h=2),
                                              stout[:, d, :, :]).then_inc(out_sem[4 + d], 16)
                    elif kind == "silu_z":
                        for m in range(TILES):
                            act.wait_ge(*taken(("row", l, m, 2)))
                        act.activation(z, z, ACT.Silu).then_inc(sig["zs"], 1)
                    elif kind == "scores":
                        u = arg[0]
                        m, t, h = HEADS[u]
                        w = P if m == 0 else TOK
                        key = ("scores", l, u)
                        act.wait_ge(sig["nb"], per["nb"] * l + u + 1)
                        act.wait_ge(*full(key))
                        src = bank(key)
                        if u >= 4:
                            act.wait_ge(*full(("turn", l, u - 4)))
                        ins = act.activation(probs[:, u % 4, 0:w], src[:, 0:w], ACT.Exp, bias=att[:, 1, u:u + 1],
                                             scale=SCALE, accum_out=att[:, 2, u:u + 1])
                        ins.then_inc(*was_read(key))
                        if t == 0:
                            act.activation(att[:, 3, u:u + 1], nsink[:, l, h:h + 1], ACT.Exp,
                                                        bias=att[:, 1, u:u + 1], scale=-1.0).then_inc(sig["es"], 1)
                    elif kind == "turn" and HEADS[arg[0]][1] == 1:
                        turn_probs(act, act.copy, l, arg[0])
                    elif kind == "gate":
                        act.wait_ge(sig["yz"], per["yz"] * l + 1)
                        for m in range(TILES):
                            ins = act.activation(tmp[:, m, :], y[:, m, :], ACT.Square, accum_out=nrm[:, 24 + m:25 + m])
                        ins.then_inc(act_step, 1)
                        act.wait_ge(act_step, act_steps())
                        act.activation(nrm[:, 27:30], nrm[:, 24:27], ACT.Ln, bias=eps_col, scale=1.0 / DS).then_inc(act_step, 1)
                        act.wait_ge(act_step, act_steps())
                        act.activation(nrm[:, 27:30], nrm[:, 27:30], ACT.Exp, scale=-0.5).then_inc(sig["yrs"], 1)
                    elif kind == "turn_mix":
                        for c in range(4):
                            key = ("mix", l, c)
                            act.wait_ge(*full(key))
                            src = bank(key)
                            act.copy(hT[:, c, :], src[:, 0:TOK]).then_inc(*was_read(key))
                        for c in range(4, KD):
                            key = ("mix", l, c)
                            act.wait_ge(*full(key))
                            src = bank(key)
                            g = pcol[:, l * N_PROW + R_SG + c - 4:l * N_PROW + R_SG + c - 3]
                            act.activation(hT[:, c, :], src[:, 0:TOK], ACT.Copy, scale=g).then_inc(*was_read(key))
                    elif kind == "router":
                        key = ("logitsT", l)
                        act.wait_ge(*full(key))
                        src = bank(key)
                        act.copy(lgT, src[0:NG + NE, 0:TOK]).then_inc(*was_read(key))
                        act.wait_ge(sig["ge0"], per["ge0"] * l + 1)
                        act.activation(rt[:, 2, :, :], rt[:, 2, :, :], ACT.Exp).then_inc(sig["ge"], 1)
                        act.wait_ge(sig["ed0"], per["ed0"] * l + 1)
                        act.activation(rt[:, 3, :, 0:1], rt[:, 3, :, 0:1], ACT.Exp).then_inc(sig["ed"], 1)
                    elif kind == "hrow":
                        for m in range(TILES):
                            for half in range(2):
                                act.wait_ge(*full(("hrow", l, m, half)))
                                src = bank(("hrow", l, m, half)).rearrange("p (a t) -> p a t", t=8)
                                dst = h_hi[:, m, :, 64 * half:64 * half + 64].rearrange("p t a -> p a t")
                                act.copy(dst, src).then_inc(sig["hhi"], 1)
                    elif kind == "more":
                        act.wait_ge(sig["flag"], l + 1)
                        over = act.value_load(flag[0:1, l:l + 1], min_val=0, max_val=1)
                        with act.If(over != 0):
                            for kind, *arg in more_steps():
                                moe(l, kind, arg)
                            for c in range(KD):
                                act.wait_ge(*taken(("sc", l, PASSES - 1, c)))
                    else:
                        moe(l, kind, arg)
            norm(DEPTH, 0)
            for m in range(TILES):
                for half in range(2):
                    key = ("out", m, half)
                    act.wait_ge(*full(key))
                    src = bank(key)
                    act.copy(row[:, m, half * 512:(half + 1) * 512], src).then_inc(*was_read(key))

        @block.vector
        def _(dve):

            tt, ts, stt = dve.tensor_tensor, dve.tensor_scalar, dve.scalar_tensor_tensor

            dve.memset(eps_col, EPS)
            dve.memset(one_col, 1.0).then_inc(dve_step, 1)
            dve.wait_ge(dve_step, dve_steps())
            dve.wait_ge(const_in, 16)
            dve.tensor_copy(ident_b, c_("ident"))
            dve.tensor_copy(mask_b, const[:, C_MASK:C_MASK + 2 * DEC].rearrange("p (b k) -> p b k", b=2))\
                .then_inc(setup_dve, 1)
            dve.memset(silu_c, 0.0).then_inc(dve_step, 1)
            dve.wait_ge(dve_step, dve_steps())
            for c in range(KD):
                key = ("xin", c)
                dve.wait_ge(*full(key))
                src = bank(key)
                dve.tensor_copy(xT[:, c, :], src[:, 0:TOK]).then_inc(*was_read(key))
            key = ("ccol",)
            dve.wait_ge(*full(key))
            src = bank(key)
            dve.tensor_copy(pcol[:, 2 * N_PROW:2 * N_PROW + 24], src[:, 0:24]).then_inc(*was_read(key))
            dve.wait_ge(*taken(key))
            dve.sem_inc(cols_ready, 1)
            dve.wait_ge(setup_act, 1)
            ts(small[:, 0:16], small[:, 0:16], 1.0, None, ALU.add).then_inc(dve_step, 1)
            dve.wait_ge(dve_step, dve_steps())
            dve.reciprocal(small[:, 16:32], small[:, 0:16]).then_inc(dve_step, 1)
            dve.wait_ge(dve_step, dve_steps())
            tt(silu_c[:, :, 0:2].rearrange("p k j -> p j k"), pcol[:, 2 * N_PROW + 8:2 * N_PROW + 24].rearrange("p (j k) -> p j k", j=2),
               small[:, 16:32].rearrange("p (j k) -> p j k", j=2), ALU.mult).then_inc(siluc_ready, 1)
            key = ("pcol",)
            dve.wait_ge(*full(key))
            src = bank(key)
            dve.tensor_copy(pcol[:, 0:2 * N_PROW], src[:, 0:2 * N_PROW]).then_inc(*was_read(key))
            dve.wait_ge(*taken(key))

            def ada(l, t):
                key = ("adaT", l, t)
                dve.wait_ge(*full(key))
                src = bank(key).rearrange("p (i q j) -> p q i j", i=4, q=4)[:, :, :, 0:2]
                bias = pcol[:, l * N_PROW + R_BADA + 16 * t:l * N_PROW + R_BADA + 16 * (t + 1)]
                tt(mods[:, l, 16 * t:16 * (t + 1), :].rearrange("p (q i) j -> p q i j", q=4), src,
                   bias.rearrange("p (q i) -> p q i", q=4).unsqueeze(3).to_broadcast((P, 4, 4, 2)), ALU.add).then_inc(*was_read(key))
                dve.wait_ge(*taken(key))
                if t != 1:
                    n = t // 2
                    sc = (SC1, SC2)[n]
                    gain = pcol[:, l * N_PROW + (R_N1, R_N2)[n]:l * N_PROW + (R_N1, R_N2)[n] + KD]
                    stt(amul[:, l, n, :, :], mods[:, l, sc:sc + KD, :], 1.0,
                             gain.unsqueeze(2).to_broadcast((P, KD, 2)), ALU.add, ALU.mult).then_inc(dve_step, 1)
                    dve.wait_ge(dve_step, dve_steps())

            ada(0, 0)

            def norm(l, n):
                key = ("ss", l, n)
                dve.wait_ge(sig["rstd"], 2 * l + n + 1)
                dve.wait_ge(*full(key))
                src = bank(key)[:, 0:TOK].unsqueeze(1).to_broadcast((P, 4, TOK))
                for half in range(2):
                    ins = tt(hT[:, 4 * half:4 * half + 4, :], xT[:, 4 * half:4 * half + 4, :], src, ALU.mult)
                    if half:
                        ins.then_inc(*was_read(key))
                        dve.wait_ge(*taken(key))
                    else:
                        ins.then_inc(dve_step, 1)
                        dve.wait_ge(dve_step, dve_steps())
                    for c in range(4 * half, 4 * half + 4):
                        if l == DEPTH:
                            ts(hT[:, c, :], hT[:, c, :], pcol[:, 2 * N_PROW + c:2 * N_PROW + c + 1],
                                           None, ALU.mult).then_inc(sig["h"], 1)
                            continue
                        for j, part in ((0, slice(0, P)), (1, slice(P, TOK))):
                            ins = ts(hT[:, c, part], hT[:, c, part], amul[:, l, n, c, j:j + 1],
                                     mods[:, l, (SH1, SH2)[n] + c, j:j + 1], ALU.mult, ALU.add)
                        ins.then_inc(sig["h"], 1)

            def residual(key, c, l, gate):
                dve.wait_ge(*full(key))
                src = bank(key)
                for j, part in ((0, slice(0, P)), (1, slice(P, TOK))):
                    ins = stt(xT[:, c, part], src[:, part], mods[:, l, gate + c, j:j + 1], xT[:, c, part],
                              ALU.mult, ALU.add)
                ins.then_inc(*was_read(key))

            def rope(m, at):
                x = row[:, m, at:at + 6 * HD]
                cos = const[:, C_COS + HD * (m - 1):C_COS + HD * m]
                sin = const[:, C_SIN + HD * (m - 1):C_SIN + HD * m].rearrange("p (f q d) -> p f q d", f=2, q=2)
                xh = x.rearrange("p (h d) -> p h d", d=HD)
                t1, t2 = tmp[:, 0, 0:6 * HD], tmp[:, 1, 0:6 * HD]
                tt(t1.rearrange("p (h d) -> p h d", d=HD), xh, cos.unsqueeze(1).to_broadcast((P, 6, HD)), ALU.mult)
                xq = x.rearrange("p (h f q d) -> p h f q d", h=6, f=2, q=2)
                tq = t2.rearrange("p (h f q d) -> p h f q d", h=6, f=2, q=2)
                for q in range(2):
                    ins = tt(tq[:, :, :, q, :], xq[:, :, :, 1 - q, :],
                             sin[:, :, q, :].unsqueeze(1).to_broadcast((P, 6, 2, 16)), ALU.mult)
                ins.then_inc(dve_step, 1)
                dve.wait_ge(dve_step, dve_steps())
                return tt(x, t1, t2, ALU.add)

            def first_of(out, eq, scratch, mi):
                iota4 = c_("iota", 4).unsqueeze(1).to_broadcast((P, TILES, 4))
                stt(scratch, eq, -100.0, iota4, ALU.mult, ALU.add).then_inc(dve_step, 1)
                dve.wait_ge(dve_step, dve_steps())
                dve.tensor_reduce(mi, scratch, AX.X, ALU.min).then_inc(dve_step, 1)
                dve.wait_ge(dve_step, dve_steps())
                return tt(out, scratch, mi.to_broadcast((P, TILES, 4)), ALU.is_equal)

            def moe(l, kind, arg):
                if kind == "select":
                    p = arg[0]
                    if p:
                        dve.wait_ge(*full(("xg", l, p - 1, KD - 1)))
                    for m in range(TILES):
                        for g in range(NG):
                            ins = ts(sel[:, m, g, :], c_("iota"), rt[:, 18 + p, m, g:g + 1], None, ALU.is_equal)
                    ins.then_inc(raised("sel", l, p), 1)
                    key = ("cwg", l, p)
                    dve.wait_ge(*full(key))
                    src = bank(key)
                    dve.tensor_copy(cwg.rearrange("p g j -> p (g j)"), src[:, 0:NE]).then_inc(*was_read(key))
                    dve.wait_ge(*taken(key))
                elif kind == "gather":
                    p = arg[0]
                    for t in range(1, KD, 2):
                        gathered(dve, dve.tensor_copy, l, p, t)
                elif kind == "gu":
                    p, e = arg
                    key = ("gu", l, p, e)
                    dve.wait_ge(raised("sgl", l, p), times("sgl", l, p, e + 1))
                    if e >= 2:
                        dve.wait_ge(*full(("hidT", l, p, e - 2)))
                    src = psum[:, uses[key][0], :]
                    stt(hid[:, e % 2, :], sg[:, e % 2, :], cwg[:, e // EPG, e % EPG:e % EPG + 1],
                                      src[:, FE:2 * FE], ALU.mult, ALU.mult).then_inc(*was_read(key))
                elif kind == "split":
                    p, e = arg
                    for half in range(2):
                        part = slice(half * D, (half + 1) * D)
                        w = slot(("down", l, p, e))[:, part]
                        dve.wait_ge(raised("whi", l, p), times("whi", l, p, 2 * e + half + 1))
                        ins = tt(down_lo[half], w, down_hi[:, part].bitcast(F32), ALU.subtract)
                    ins.then_inc(raised("wlo", l, p), 1)
                elif kind == "turn_hid":
                    p, e = arg
                    key = ("hidT", l, p, e)
                    dve.wait_ge(raised("hthi", l, p), times("hthi", l, p, e + 1))
                    tt(hidT_lo[:, e % 2, :], bank(key)[:, 0:2 * P], hidT[:, e % 2, :].bitcast(F32), ALU.subtract)\
                        .then_inc(*was_read(key))
                elif kind == "down":
                    p, e = arg
                    if e % EPG == EPG - 1:
                        g = e // EPG
                        for half in range(2):
                            key = ("yg", l, p, g, half)
                            part = slice(half * 512, (half + 1) * 512)
                            dve.wait_ge(raised("yhi", l, p), times("yhi", l, p, 2 * g + half + 1))
                            tt(y_lo[:, g, part], psum[:, uses[key][0], :],
                                             y_hi[:, g, part].bitcast(F32), ALU.subtract).then_inc(*was_read(key))
                elif kind == "scatter":
                    for c in range(KD):
                        residual(("sc", l, arg[0], c), c, l, G2)

            for l in range(DEPTH):
                for step in STEPS[l]:
                    kind, arg = step[0], step[1:]
                    if kind == "norm":
                        norm(l, arg[0])
                    elif kind == "ada_turn":
                        ada(*arg)
                    elif kind == "xbc":
                        if l == 0:
                            dve.wait_ge(tab_in, 16 * 8 * DEPTH)
                            ts(nsink, tab[:, :, T_SINK:T_SINK + NH], -1.0, None, ALU.mult).then_inc(dve_step, 1)
                            dve.wait_ge(dve_step, dve_steps())
                        key = ("dt", l)
                        dve.wait_ge(*full(key))
                        src = bank(key)
                        bias = tab[:, l, T_DTB:T_DTB + DT].unsqueeze(1).to_broadcast((P, TILES, DT))
                        tt(dtw[:, 0, :].rearrange("p (m n) -> p m n", n=DT),
                                         src[:, 0:TILES * DT].rearrange("p (m n) -> p m n", n=DT), bias, ALU.add).then_inc(*was_read(key))
                        dve.wait_ge(*taken(key))
                        stt(dtw[:, 1, :], dtw[:, 0, :], -1.0, dtw[:, 0, :], ALU.mult, ALU.min).then_inc(sig["dt_na"], 1)
                        for c in range(6):
                            key = ("xbc", l, c)
                            dve.wait_ge(*full(key))
                            src = bank(key)
                            cw = [pcol[:, l * N_PROW + R_CW + 6 * t + c:l * N_PROW + R_CW + 6 * t + c + 1] for t in range(3)]
                            cb = pcol[:, l * N_PROW + R_CB + c:l * N_PROW + R_CB + c + 1]
                            ts(xbc[:, c, :], src[:, 0:TOK], cw[1], cb, ALU.mult, ALU.add).then_inc(dve_step, 1)
                            dve.wait_ge(dve_step, dve_steps())
                            for b0, b1 in ((0, P), (P, TOK)):
                                ins = stt(xbc[:, c, b0 + 1:b1], src[:, b0:b1 - 1], cw[0], xbc[:, c, b0 + 1:b1],
                                          ALU.mult, ALU.add)
                            ins.then_inc(dve_step, 1)
                            dve.wait_ge(dve_step, dve_steps())
                            stt(xbc[:, c, 0:P - 1], src[:, 1:P], cw[2], xbc[:, c, 0:P - 1], ALU.mult, ALU.add)
                            stt(xbc[:, c, P:TOK - 1], src[:, P + 1:TOK], cw[2], xbc[:, c, P:TOK - 1],
                                              ALU.mult, ALU.add).then_inc(*was_read(key))
                        dve.wait_ge(sig["dt_u"], per["dt_u"] * l + 1)
                        ts(dtw[:, 3, :], dtw[:, 1, :], 1.0, -1.0, ALU.add, ALU.add)
                        ts(dtw[:, 4, :], dtw[:, 1, :], 1.0, None, ALU.add).then_inc(dve_step, 1)
                        dve.wait_ge(dve_step, dve_steps())
                        tt(dtw[:, 3, :], dtw[:, 1, :], dtw[:, 3, :], ALU.subtract)
                        dve.reciprocal(dtw[:, 5, :], dtw[:, 4, :]).then_inc(dve_step, 1)
                        dve.wait_ge(dve_step, dve_steps())
                        tt(dtw[:, 3, :], dtw[:, 3, :], dtw[:, 5, :], ALU.mult).then_inc(dve_step, 1)
                        dve.wait_ge(dve_step, dve_steps())
                        dve.wait_ge(sig["dt_r"], per["dt_r"] * l + 1)
                        tt(dtw[:, 3, :], dtw[:, 3, :], dtw[:, 2, :], ALU.add).then_inc(dve_step, 1)
                        dve.wait_ge(dve_step, dve_steps())
                        stt(dts.rearrange("p m n -> p (m n)"), dtw[:, 0, :], 0.0, dtw[:, 3, :], ALU.max, ALU.add).then_inc(dve_step, 1)
                        dve.wait_ge(dve_step, dve_steps())
                        if l == 0:
                            dve.wait_ge(setup_act, 2)
                        stt(dav, dts, -1.0, a_exp[:, l, :].unsqueeze(1).to_broadcast((P, TILES, DT)),
                                         ALU.mult, ALU.mult).then_inc(sig["da"], 1)
                    elif kind == "caches":
                        for lc in range(DEPTH):
                            key = ("ck", lc)
                            dve.wait_ge(*full(key))
                            src = bank(key)
                            dve.tensor_copy(ckT[:, lc, :, :].rearrange("p t s -> p (t s)"), src[:, 0:2 * P])\
                                .then_inc(*was_read(key))
                            key = ("h0", lc)
                            dve.wait_ge(*full(key))
                            src = bank(key)
                            dve.tensor_copy(h0T[:, lc, :, :].rearrange("p t s -> p (t s)"), src).then_inc(*was_read(key))
                    elif kind == "prep":
                        m = arg[0]
                        dve.wait_ge(*taken(("row", l, m, 0)))
                        dve.wait_ge(*taken(("row", l, m, 1)))
                        b6 = row[:, m, OFF_B:OFF_B + 6 * HD]
                        b6h = b6.rearrange("p (h d) -> p h d", d=HD)
                        tt(tmp[:, 2, 0:6 * HD], b6, b6, ALU.mult).then_inc(dve_step, 1)
                        dve.wait_ge(dve_step, dve_steps())
                        dve.tensor_reduce(nrm[:, 0:6], tmp[:, 2, 0:6 * HD].rearrange("p (h d) -> p h d", d=HD),
                                                        AX.X, ALU.add).then_inc(sig["bss"], 1)
                        if m:
                            rope(m, 0).then_inc(dve_step, 1)
                            dve.wait_ge(dve_step, dve_steps())
                        dve.wait_ge(sig["brs"], per["brs"] * l + m + 1)
                        tt(b6h, b6h, nrm[:, 16:22].unsqueeze(2).to_broadcast((P, 6, HD)), ALU.mult).then_inc(dve_step, 1)
                        dve.wait_ge(dve_step, dve_steps())
                        ins = tt(b6, b6, tab[:, l, T_GQK:T_GQK + 6 * HD], ALU.mult)
                        if m:
                            ins.then_inc(dve_step, 1)
                            dve.wait_ge(dve_step, dve_steps())
                            ins = rope(m, OFF_B)
                        ins.then_inc(sig["prep"], 1)
                    elif kind == "ssm_in":
                        m = arg[0]
                        key = ("bg", l, m)
                        dve.wait_ge(*full(key))
                        src = bank(key)
                        if m:
                            dve.wait_ge(*full(("state", l, m - 1)))
                        dve.tensor_copy(bro, src[:, 0:P])
                        for g in range(2):
                            if g:
                                key = ("bg1", l, m)
                                dve.wait_ge(*full(key))
                                src = bank(key)
                            tt(gm[:, 0, g, :], src[:, P:2 * P], c_("incl_f"), ALU.mult)
                            tt(gm[:, 1, g, :], src[:, P:2 * P], c_("incl_b"), ALU.mult).then_inc(*was_read(key))
                    elif kind == "seg":
                        m = arg[0]
                        dve.wait_ge(*taken(("bg", l, m)))
                        dve.wait_ge(*taken(("bg1", l, m)))
                        for d in range(2):
                            for g in range(2):
                                key = ("seg", l, m, d, g)
                                dve.wait_ge(sig["seg"], per["seg"] * l + 4 * m + 2 * d + g + 1)
                                src = psum[:, uses[key][0], :].rearrange("p (h t) -> p h t", h=4)
                                tt(mm[:, d, 4 * g:4 * g + 4, :], src,
                                                 gm[:, d, g, :].unsqueeze(1).to_broadcast((P, 4, P)), ALU.mult).then_inc(*was_read(key))
                    elif kind == "ssm_y":
                        m = arg[0]
                        key = ("ydiag", l, m)
                        dve.wait_ge(sig["yx"], per["yx"] * l + m + 1)
                        dve.wait_ge(*full(key))
                        src = bank(key)
                        tt(y[:, m, :], src, yx, ALU.add).then_inc(*was_read(key))
                        if m:
                            d = m - 1
                            key = ("state", l, m)
                            dve.wait_ge(*taken(("cum", l, m)))
                            dve.wait_ge(*taken(("h0", l)))
                            for g in range(2):
                                part = slice(64 * g, 64 * g + 64)
                                total = ex[part, m, 32 + 8 * d + 4 * g:32 + 8 * d + 4 * g + 4]
                                ins = tt(hin[part, d, :].rearrange("p (h n) -> p h n", h=4),
                                         h0T[part, l, d, :].rearrange("p (h n) -> p h n", h=4),
                                         total.unsqueeze(2).to_broadcast((64, 4, HD)), ALU.mult)
                            ins.then_inc(dve_step, 1)
                            dve.wait_ge(dve_step, dve_steps())
                            dve.wait_ge(*full(key))
                            src = bank(key)
                            tt(hin[:, d, :], src[:, 0:256], hin[:, d, :], ALU.add).then_inc(*was_read(key))
                    elif kind == "ssm_off":
                        m = arg[0]
                        dve.wait_ge(*taken(("ydiag", l, m)))
                        for g in range(2):
                            key = ("yoff", l, m, g)
                            dve.wait_ge(*full(key))
                            src = bank(key).rearrange("p (d h n) -> p d h n", d=2, h=4)
                            dec = ex[:, m, 0:16].rearrange("p (d h) -> p d h", d=2)[:, :, 4 * g:4 * g + 4]
                            tt(tmp[:, g, :].rearrange("p (d h n) -> p d h n", d=2, h=4), src,
                                             dec.unsqueeze(3).to_broadcast((P, 2, 4, HD)), ALU.mult).then_inc(*was_read(key))
                        dve.wait_ge(*taken(("yoff", l, m, 0)))
                        dve.wait_ge(*taken(("yoff", l, m, 1)))
                        ym = y[:, m, :].rearrange("p (g n) -> p g n", g=2)
                        for d in range(2):
                            tt(ym, ym, tmp[:, 0:2, d * 256:(d + 1) * 256], ALU.add).then_inc(dve_step, 1)
                            dve.wait_ge(dve_step, dve_steps())
                    elif kind == "scores":
                        u = arg[0]
                        m, t, h = HEADS[u]
                        dve.wait_ge(*full(("scores", l, u)))
                        src = bank(("scores", l, u))
                        dve.tensor_reduce(att[:, 0, u:u + 1], src[:, 0:P if m == 0 else TOK], AX.X, ALU.max,
                                               negate=True).then_inc(dve_step, 1)
                        dve.wait_ge(dve_step, dve_steps())
                        if t == 0:
                            ins = ts(att[:, 1, u:u + 1], att[:, 0, u:u + 1], SCALE, nsink[:, l, h:h + 1],
                                     ALU.mult, ALU.min)
                        else:
                            ins = ts(att[:, 1, u:u + 1], att[:, 0, u:u + 1], SCALE, None, ALU.mult)
                        ins.then_inc(sig["nb"], 1)
                    elif kind == "turn" and HEADS[arg[0]][1] == 0:
                        turn_probs(dve, dve.tensor_copy, l, arg[0])
                    elif kind == "values":
                        u = arg[0]
                        m, t, h = HEADS[u]
                        den = att[:, 2, u:u + 1]
                        if t == 0:
                            dve.wait_ge(sig["es"], per["es"] * l + sum(1 for x in HEADS[:u + 1] if x[1] == 0))
                            tt(att[:, 4, u:u + 1], den, att[:, 3, u:u + 1], ALU.add).then_inc(dve_step, 1)
                            dve.wait_ge(dve_step, dve_steps())
                            den = att[:, 4, u:u + 1]
                        else:
                            dve.wait_ge(*taken(("scores", l, u)))
                        dve.reciprocal(att[:, 5, u:u + 1], den).then_inc(dve_step, 1)
                        dve.wait_ge(dve_step, dve_steps())
                        key = ("values", l, u)
                        dve.wait_ge(*full(key))
                        src = bank(key)
                        ts(row[:, m, t * OFF_B + h * HD:t * OFF_B + (h + 1) * HD], src[:, 0:HD],
                                         att[:, 5, u:u + 1], None, ALU.mult).then_inc(*was_read(key))
                    elif kind == "gate":
                        dve.wait_ge(sig["zs"], per["zs"] * l + 1)
                        dve.wait_ge(*taken(("ydiag", l, 0)))
                        tt(y, y, z, ALU.mult).then_inc(sig["yz"], 1)
                        dve.wait_ge(sig["yrs"], per["yrs"] * l + 1)
                        for m in range(TILES):
                            ins = ts(y[:, m, :], y[:, m, :], nrm[:, 27 + m:28 + m], None, ALU.mult)
                        ins.then_inc(sig["yn"], 1)
                    elif kind == "wout":
                        for c in range(KD):
                            residual(("wout", l, c), c, l, G1)
                    elif kind == "router":
                        key = ("logits", l)
                        dve.wait_ge(*full(key))
                        src = bank(key)
                        n = NG + NE
                        bias = tab[:, l, T_BG:T_BG + n].unsqueeze(1).to_broadcast((P, TILES, n))
                        tt(lg, src[:, 0:TILES * n].rearrange("p (m n) -> p m n", n=n), bias, ALU.add).then_inc(*was_read(key))
                        dve.wait_ge(*taken(key))
                        col = lambda i, j: rt[:, i, :, j:j + 1]
                        bc = lambda v: v.to_broadcast((P, TILES, 4))
                        dve.tensor_reduce(col(6, 0), lg[:, :, 0:NG], AX.X, ALU.max).then_inc(dve_step, 1)
                        dve.wait_ge(dve_step, dve_steps())
                        tt(rt[:, 2, :, :], lg[:, :, 0:NG], bc(col(6, 0)), ALU.subtract).then_inc(sig["ge0"], 1)
                        tt(rt[:, 8, :, :], lg[:, :, 0:NG], bc(col(6, 0)), ALU.is_equal).then_inc(dve_step, 1)
                        dve.wait_ge(dve_step, dve_steps())
                        first_of(rt[:, 0, :, :], rt[:, 8, :, :], rt[:, 9, :, :], col(6, 1)).then_inc(sig["goh"], 1)
                        dve.wait_ge(sig["goh"], per["goh"] * l + 1)
                        tt(e16.rearrange("p m (g j) -> p m g j", g=NG),
                                lg[:, :, NG:n].rearrange("p m (g j) -> p m g j", g=NG),
                                rt[:, 0, :, :].unsqueeze(3).to_broadcast((P, TILES, NG, EPG)), ALU.mult).then_inc(dve_step, 1)
                        dve.wait_ge(dve_step, dve_steps())
                        dve.tensor_reduce(rt[:, 10, :, :], e16.rearrange("p m (g j) -> p m j g", g=NG), AX.X, ALU.add).then_inc(dve_step, 1)
                        dve.wait_ge(dve_step, dve_steps())
                        dve.tensor_reduce(col(6, 2), rt[:, 10, :, :], AX.X, ALU.max).then_inc(dve_step, 1)
                        dve.wait_ge(dve_step, dve_steps())
                        tt(rt[:, 8, :, :], rt[:, 10, :, :], bc(col(6, 2)), ALU.is_equal).then_inc(dve_step, 1)
                        dve.wait_ge(dve_step, dve_steps())
                        first_of(rt[:, 11, :, :], rt[:, 8, :, :], rt[:, 9, :, :], col(6, 3)).then_inc(dve_step, 1)
                        dve.wait_ge(dve_step, dve_steps())
                        stt(rt[:, 12, :, :], rt[:, 11, :, :], -BIG, rt[:, 10, :, :], ALU.mult, ALU.add).then_inc(dve_step, 1)
                        dve.wait_ge(dve_step, dve_steps())
                        dve.tensor_reduce(col(13, 0), rt[:, 12, :, :], AX.X, ALU.max).then_inc(dve_step, 1)
                        dve.wait_ge(dve_step, dve_steps())
                        tt(col(3, 0), col(13, 0), col(6, 2), ALU.subtract).then_inc(sig["ed0"], 1)
                        tt(rt[:, 8, :, :], rt[:, 12, :, :], bc(col(13, 0)), ALU.is_equal).then_inc(dve_step, 1)
                        dve.wait_ge(dve_step, dve_steps())
                        first_of(rt[:, 14, :, :], rt[:, 8, :, :], rt[:, 9, :, :], col(13, 1)).then_inc(dve_step, 1)
                        dve.wait_ge(dve_step, dve_steps())
                        dve.wait_ge(sig["ge"], per["ge"] * l + 1)
                        dve.tensor_reduce(col(13, 2), rt[:, 2, :, :], AX.X, ALU.add).then_inc(dve_step, 1)
                        dve.wait_ge(dve_step, dve_steps())
                        dve.wait_ge(sig["ed"], per["ed"] * l + 1)
                        stt(col(15, 0), col(3, 0), 1.0, col(13, 2), ALU.add, ALU.mult).then_inc(dve_step, 1)
                        dve.wait_ge(dve_step, dve_steps())
                        dve.reciprocal(col(15, 1), col(15, 0)).then_inc(dve_step, 1)
                        dve.wait_ge(dve_step, dve_steps())
                        tt(col(15, 2), col(15, 1), col(3, 0), ALU.mult).then_inc(dve_step, 1)
                        dve.wait_ge(dve_step, dve_steps())
                        tt(rt[:, 16, :, :], rt[:, 11, :, :], bc(col(15, 1)), ALU.mult)
                        tt(rt[:, 17, :, :], rt[:, 14, :, :], bc(col(15, 2)), ALU.mult).then_inc(dve_step, 1)
                        dve.wait_ge(dve_step, dve_steps())
                        tt(rt[:, 1, :, :], rt[:, 16, :, :], rt[:, 17, :, :], ALU.add).then_inc(sig["cw"], 1)
                    elif kind == "hrow":
                        for m in range(TILES):
                            for half in range(2):
                                key = ("hrow", l, m, half)
                                dve.wait_ge(sig["hhi"], per["hhi"] * l + 2 * m + half + 1)
                                dve.wait_ge(*full(key))
                                src = bank(key).rearrange("p (a t) -> p a t", t=8)
                                part = slice(64 * half, 64 * half + 64)
                                tt(h_lo[:, m, :, part].rearrange("p t a -> p a t"), src,
                                                 h_hi[:, m, :, part].bitcast(F32).rearrange("p t a -> p a t"),
                                                 ALU.subtract).then_inc(*was_read(key))
                    elif kind == "rank":
                        key = ("rank", l)
                        dve.wait_ge(*full(key))
                        src = bank(key)[:, 0:TILES * NG].rearrange("p (m g) -> p m g", g=NG)
                        dve.tensor_reduce(rt[:, 5, 0, 0:1], bank(key)[:, TILES * NG:(TILES + 1) * NG], AX.X, ALU.max)\
                            .then_inc(dve_step, 1)
                        dve.wait_ge(dve_step, dve_steps())
                        ts(flag[:, l:l + 1], rt[:, 5, 0, 0:1], float(P), None, ALU.is_gt).then_inc(sig["flag"], 1)
                        stt(rt[:, 4, :, :], src, 1.0, rt[:, 0, :, :], ALU.add, ALU.mult).then_inc(*was_read(key))
                        dve.wait_ge(*taken(key))
                        for p in range(PASSES):
                            ins = ts(rt[:, 18 + p, :, :], rt[:, 4, :, :], -1.0 - P * p, None, ALU.add)
                        ins.then_inc(dve_step, 1)
                        dve.wait_ge(dve_step, dve_steps())
                    elif kind == "more":
                        dve.wait_ge(sig["flag"], l + 1)
                        over = dve.value_load(flag[0:1, l:l + 1], min_val=0, max_val=1)
                        with dve.If(over != 0):
                            for kind, *arg in more_steps():
                                moe(l, kind, arg)
                    else:
                        moe(l, kind, arg)
            norm(DEPTH, 0)

        @block.gpsimd
        def _(pool):

            tt = pool.tensor_tensor
            pool.wait_ge(const_in, 16)
            pool.wait_ge(tab_in, 16 * 8 * DEPTH)
            for l in range(DEPTH):
                for step in STEPS[l]:
                    if step[0] != "ssm_in":
                        continue
                    m = step[1]
                    pool.wait_ge(sig["da"], per["da"] * l + 1)
                    if m:
                        pool.wait_ge(*full(("seg", l, m - 1, 1, 1)))
                    for d, tri in enumerate(("incl_f", "incl_b")):
                        ins = tt(ud[:, d, :, :], c_(tri).unsqueeze(1).to_broadcast((P, SH, P)),
                                 dav[:, m, 8 * d:8 * d + 8].unsqueeze(2).to_broadcast((P, SH, P)), ALU.mult)
                    ins.then_inc(sig["ud"], 1)
                    pool.wait_ge(*taken(("xs", l, m)))
                    pool.wait_ge(*taken(("cum", l, m)))
                    if m:
                        pool.wait_ge(*taken(("ydiag", l, m - 1)))
                    xh = xs.rearrange("p (h n) -> p h n", h=SH)
                    tt(yx.rearrange("p (h n) -> p h n", h=SH), xh,
                                    tab[:, l, T_DSK:T_DSK + SH].unsqueeze(2).to_broadcast((P, SH, HD)), ALU.mult).then_inc(sig["yx"], 1)
                    if m:
                        pool.wait_ge(*full(("state", l, m - 1)))
                    for d in range(2):
                        ins = tt(xd[:, d, :, :], xh,
                                 dts[:, m, 8 * d:8 * d + 8].unsqueeze(2).to_broadcast((P, SH, HD)), ALU.mult)
                    ins.then_inc(pool_step, 1)
                    pool.wait_ge(pool_step, pool_steps())
                    for d in range(2):
                        ins = tt(xdd[:, d, :, :], xd[:, d, :, :],
                                 ex[:, m, 16 + 8 * d:24 + 8 * d].unsqueeze(2).to_broadcast((P, SH, HD)), ALU.mult)
                    ins.then_inc(sig["xd"], 1)


_INS = ["x_prompt", "x_sample", "cache_a_k", "cache_a_v", "cache_b_k", "cache_b_v", "state_ssm_fwd",
        "state_ssm_bwd", "c", "c_ctx", "norm1_g", "norm2_g", "final_norm_g", "w_ada", "b_ada", "w_in", "a_sink",
        "q_norm_g", "k_norm_g", "conv_w", "conv_b", "dt_bias", "a_log", "d_skip", "ssm_norm_g", "w_out",
        "w_router_group", "b_router_group", "w_router_expert", "b_router_expert", "w_gate", "w_up", "w_down"]
_OUTS = [(1, SEQ, D), (1, DEC, D)] + [(1, DEPTH, SEQ, NKV, HD)] * 4 + [(1, DEPTH, SH, HD, 64)] * 2


def kernel(**inputs):
    import concourse.bacc as bacc
    from concourse.bass_utils import run_bass_kernel_spmd as run

    nc = bacc.Bacc("TRN2", target_bir_lowering=False, num_devices=1)
    arrays = {n: np.ascontiguousarray(inputs[n]) for n in _INS}
    arrays["const"] = constants()
    a = {n: nc.dram_tensor("in_" + n, v.shape, F32, kind="ExternalInput").ap() for n, v in arrays.items()}
    outs = [nc.dram_tensor(f"out_{i}", s, F32, kind="ExternalOutput").ap() for i, s in enumerate(_OUTS)]
    build(nc, a, outs)
    r = run(nc, [{"in_" + n: v for n, v in arrays.items()}], core_ids=[0])
    return tuple(r.results[0][f"out_{i}"] for i in range(len(_OUTS)))
```
